# Optimizing a Trainium2 kernel written in Bass

```python
import jax, jax.numpy as jnp
from jax import lax
import numpy as np

D_MODEL = 2048
BATCH = 1
SEQ = 256
DEPTH = 1

D_MIX = D_MODEL
D_CONF = D_MIX // 2
D_SC = D_MIX - D_CONF
CONF_KERNEL = 31
SC_KERNEL = 3
D_IN_PROJ = 2 * D_CONF + 3 * D_SC
PEER_HEADS = 8
N_KEYS = 128
N_EXPERTS = N_KEYS * N_KEYS
D_KEY = 256
D_HALF = D_KEY // 2
TOPK_HALF = 16
TOPK = 16
TOKEN_BLOCK = 128
LN_EPS = 1e-5
DEEPNORM_ALPHA = (2.0 * DEPTH) ** 0.25
DEEPNORM_BETA = (8.0 * DEPTH) ** -0.25

kernel_name = 'hybrid_conformer_shortconv_peer_layer'

def layer_norm(x, g, b):
    xf = x.astype(jnp.float32)
    mu = jnp.mean(xf, axis=-1, keepdims=True)
    var = jnp.mean(jnp.square(xf - mu), axis=-1, keepdims=True)
    y = (xf - mu) * lax.rsqrt(var + LN_EPS) * g.astype(jnp.float32) + b.astype(jnp.float32)
    return y.astype(x.dtype)

def causal_depthwise_conv(x, w, b):
    k, c = w.shape
    y = lax.conv_general_dilated(
        x, w[:, None, :].astype(x.dtype), window_strides=(1,), padding=[(k - 1, 0)],
        dimension_numbers=('NWC', 'WIO', 'NWC'), feature_group_count=c)
    return y + b

def peer_block(x_tok, w_q, sub_keys, peer_u, peer_v):
    t = x_tok.shape[0]
    q = (x_tok @ w_q).reshape(t, PEER_HEADS, 2, D_HALF)
    s = jnp.einsum('thpc,hpnc->thpn', q, sub_keys).astype(jnp.float32)
    s1, i1 = lax.top_k(s[:, :, 0], TOPK_HALF)
    s2, i2 = lax.top_k(s[:, :, 1], TOPK_HALF)
    cand = (s1[..., :, None] + s2[..., None, :]).reshape(t, PEER_HEADS, TOPK_HALF * TOPK_HALF)
    top_s, ci = lax.top_k(cand, TOPK)
    e1 = jnp.take_along_axis(i1, ci // TOPK_HALF, axis=-1)
    e2 = jnp.take_along_axis(i2, ci % TOPK_HALF, axis=-1)
    experts = e1 * N_KEYS + e2
    g = jax.nn.softmax(top_s, axis=-1)
    u_sel = peer_u[experts]
    act = jax.nn.gelu(jnp.einsum('td,thkd->thk', x_tok, u_sel), approximate=False)
    coef = act * g.astype(act.dtype)
    v_sel = peer_v[experts]
    return jnp.einsum('thk,thkd->td', coef, v_sel)

def setup_inputs(seed: int = 0) -> dict:
    key = jax.random.key(seed)
    ks = jax.random.split(key, 20)
    f32 = jnp.float32
    L = DEPTH

    def nrm(k, shape, scale):
        return jax.random.normal(k, shape, f32) * scale

    return {
        'x': jax.random.normal(ks[0], (BATCH, SEQ, D_MODEL), f32),
        'w_in': nrm(ks[1], (L, D_MODEL, D_IN_PROJ), D_MODEL ** -0.5),
        'b_in': nrm(ks[2], (L, D_IN_PROJ), 0.02),
        'conf_conv_w': nrm(ks[3], (L, CONF_KERNEL, D_CONF), CONF_KERNEL ** -0.5),
        'conf_conv_b': nrm(ks[4], (L, D_CONF), 0.02),
        'conf_ln_g': 1.0 + nrm(ks[5], (L, D_CONF), 0.02),
        'conf_ln_b': nrm(ks[6], (L, D_CONF), 0.02),
        'sc_conv_w': nrm(ks[7], (L, SC_KERNEL, D_SC), SC_KERNEL ** -0.5),
        'sc_conv_b': nrm(ks[8], (L, D_SC), 0.02),
        'w_out': nrm(ks[9], (L, D_MIX, D_MODEL), D_MIX ** -0.5 * DEEPNORM_BETA),
        'b_out': nrm(ks[10], (L, D_MODEL), 0.02),
        'ln1_g': 1.0 + nrm(ks[11], (L, D_MODEL), 0.02),
        'ln1_b': nrm(ks[12], (L, D_MODEL), 0.02),
        'w_q': nrm(ks[13], (L, D_MODEL, PEER_HEADS * D_KEY), D_MODEL ** -0.5),
        'sub_keys': nrm(ks[14], (L, PEER_HEADS, 2, N_KEYS, D_HALF), D_HALF ** -0.5),
        'peer_u': nrm(ks[15], (L, N_EXPERTS, D_MODEL), D_MODEL ** -0.5),
        'peer_v': nrm(ks[16], (L, N_EXPERTS, D_MODEL), DEEPNORM_BETA),
        'ln2_g': 1.0 + nrm(ks[17], (L, D_MODEL), 0.02),
        'ln2_b': nrm(ks[18], (L, D_MODEL), 0.02),
    }

def reference(x, w_in, b_in, conf_conv_w, conf_conv_b, conf_ln_g, conf_ln_b,
              sc_conv_w, sc_conv_b, w_out, b_out, ln1_g, ln1_b,
              w_q, sub_keys, peer_u, peer_v, ln2_g, ln2_b):
    splits = [D_CONF, 2 * D_CONF, 2 * D_CONF + D_SC, 2 * D_CONF + 2 * D_SC]
    for l in range(DEPTH):
        h = x @ w_in[l] + b_in[l]
        a_val, a_gate, sc_b, sc_c, sc_h = jnp.split(h, splits, axis=-1)
        a = a_val * jax.nn.sigmoid(a_gate)
        a = causal_depthwise_conv(a, conf_conv_w[l], conf_conv_b[l])
        a = jax.nn.silu(layer_norm(a, conf_ln_g[l], conf_ln_b[l]))
        s = sc_b * causal_depthwise_conv(sc_c * sc_h, sc_conv_w[l], sc_conv_b[l])
        y = jnp.concatenate([a, s], axis=-1) @ w_out[l] + b_out[l]
        x = layer_norm(DEEPNORM_ALPHA * x + y, ln1_g[l], ln1_b[l])
        x_blocks = x.reshape(-1, TOKEN_BLOCK, D_MODEL)
        wq_l, sk_l, u_l, v_l = w_q[l], sub_keys[l], peer_u[l], peer_v[l]
        f = lax.map(lambda xb: peer_block(xb, wq_l, sk_l, u_l, v_l), x_blocks)
        f = f.reshape(x.shape)
        x = layer_norm(DEEPNORM_ALPHA * x + f, ln2_g[l], ln2_b[l])
    return x


_drawn_inputs = setup_inputs


def setup_inputs(seed=0):
    import zlib

    import numpy as np

    out = dict(_drawn_inputs(seed))
    spreads = {}
    factors = {'conf_ln_g': 2.901, 'conf_ln_b': 3.508, 'sc_conv_b': 2.734, 'ln2_g': 2.826, 'ln2_b': 2.842}
    for name, (base, spread) in spreads.items():
        noise = np.random.default_rng([zlib.crc32(name.encode()), seed]).standard_normal(out[name].shape)
        drawn = base * np.exp(spread * noise) if base else spread * noise
        out[name] = __import__('jax').numpy.asarray(drawn.astype(out[name].dtype))
    for name, factor in factors.items():
        out[name] = (out[name] * factor).astype(out[name].dtype)
    return out
```

```python
import concourse.bass as bass
from concourse import mybir
from contextlib import ExitStack

P = 128
T = 256
TB = T // P
D = 2048
KT = D // P
HALF = KT // 2
CONF_TILES = 8
SC_TILES = 8
TAPS = 31
SC_TAPS = 3
HEADS = 8
TOPK = 16
N_KEYS = 128
DCH = 512
NCH = D // DCH
GROUP = 4
GROUPS = N_KEYS // GROUP
QUARTER = 32
GROUPS_Q = QUARTER // GROUP
BATCH = 8
ALPHA = 2.0 ** 0.25
EPS = 1e-5
RAW = 8
SPLIT = 4
LEAD = 3

U_CONF = 0
U_SC = U_CONF + 2 * 2 * CONF_TILES
U_OUT = U_SC + 3 * 2 * SC_TILES
U_Q = U_OUT + NCH * HALF
U_PRE = U_Q + 2 * 2 * HEADS
U_MAIN = U_PRE + 2 * GROUP * 2
STEP = 4
GSTEP = GROUP * STEP
U_TAIL = U_MAIN + (GROUPS - 2) * GSTEP
U_END = U_TAIL + 2 * 2 * GROUP
PC_B = 0
PC_CW = PC_B + 2 * CONF_TILES + 3 * SC_TILES
PC_CB = PC_CW + CONF_TILES * TAPS
PC_LG = PC_CB + CONF_TILES
PC_LB = PC_LG + CONF_TILES
PC_SW = PC_LB + CONF_TILES
PC_SB = PC_SW + SC_TILES * SC_TAPS
PC_END = PC_SB + SC_TILES


def build(nc, x_t, x_nat, w_in, w_out, w_q, u_w, v_w, params, sub_keys, b_out, ln1_g, ln1_b, ln2_g, ln2_b, out):
    f32 = mybir.dt.float32
    f32r = mybir.dt.float32r
    u32 = mybir.dt.uint32
    ALU = mybir.AluOpType
    ACT = mybir.ActivationFunctionType
    AX = mybir.AxisListType
    ds = bass.ds

    ctx = ExitStack()
    with ctx:
        def sb(name, shape, dt, where=ctx):
            return where.enter_context(nc.sbuf_tensor(name, shape, dt))

        def sem(name):
            return ctx.enter_context(nc.semaphore(name))

        raw = sb("raw", [P, RAW, HALF * P], f32)
        w_hi = [sb(f"w_hi{i}", [P, HALF * P], f32r) for i in range(SPLIT)]
        w_lo = [sb(f"w_lo{i}", [P, HALF * P], f32r) for i in range(SPLIT)]
        xt_hi = sb("xt_hi", [P, KT, T], f32r)
        xt_lo = sb("xt_lo", [P, KT, T], f32r)
        acc = sb("acc", [P, TB, D], f32)
        iota = sb("iota", [P, P], f32)
        ident = sb("ident", [P, P], f32)
        stats = sb("stats", [P, TB, NCH, 6], f32)
        mv = sb("mv", [P, TB, 2], f32)
        rstd = sb("rstd", [P, TB, 1], f32)
        early = ExitStack()
        keys = sb("keys", [P, 2 * HEADS * N_KEYS], f32, early)
        xt_raw = sb("xt_raw", [P, KT, T], f32, early)
        prm = sb("prm", [P, PC_END], f32, early)
        apad = sb("apad", [P, CONF_TILES, TAPS - 1 + T], f32, early)
        cacc = sb("cacc", [P, 2, CONF_TILES, T], f32, early)
        mix_hi = sb("mix_hi", [P, KT, T], f32r, early)
        mix_lo = sb("mix_lo", [P, KT, T], f32r, early)
        scpad = sb("scpad", [P, SC_TAPS - 1 + T], f32, early)
        sct = sb("sct", [P, 2, T], f32, early)
        sig = sb("sig", [P, 2, T], f32, early)
        hval = sb("hval", [P, 2, T], f32, early)
        smix = sb("smix", [P, T], f32, early)
        ones = sb("ones", [P, P], f32, early)
        lnt = sb("lnt", [P, 2, T], f32, early)
        ln_g = xt_raw[:, 0:8, :].rearrange("p a b -> p (a b)")
        ln_b = xt_raw[:, 8:16, :].rearrange("p a b -> p (a b)")
        bo = sb("bo", [P, D], f32, early)
        early.close()
        c_hi = [sb(f"c_hi{i}", [P, GROUP, T], f32r) for i in range(2)]
        c_lo = [sb(f"c_lo{i}", [P, GROUP, T], f32r) for i in range(2)]
        tab1 = sb("tab1", [P, T], f32)
        tab2 = sb("tab2", [P, T], f32)
        gate_t = sb("gate_t", [P, 2, T], f32r)
        stash = [sb(f"stash{i}", [P, GROUP, T], f32) for i in range(2)]
        oh1 = [sb(f"oh1_{i}", [P, BATCH, P], f32r) for i in range(2)]
        oh2 = sb("oh2", [P, BATCH, QUARTER], f32)
        oh2g = [sb(f"oh2g_{i}", [P, 2, BATCH, QUARTER], f32r) for i in range(2)]
        route = ExitStack()
        q_t = [sb(f"q_t{i}", [P, T], f32, route) for i in range(2)]
        srest = sb("srest", [P, TB, N_KEYS], f32, route)
        cand = sb("cand", [P, TB, TOPK, TOPK], f32, route)
        crest = sb("crest", [P, TB, TOPK * TOPK], f32, route)
        hv = [sb(f"hv{i}", [P, TB, TOPK], f32, route) for i in range(2)]
        hidx = [sb(f"hidx{i}", [P, TB, TOPK], u32, route) for i in range(2)]
        cv = sb("cv", [P, TB, TOPK], f32, route)
        cidx = sb("cidx", [P, TB, TOPK], u32, route)
        hidx_f = sb("hidx_f", [P, TB, 2 * HEADS, TOPK], f32, route)
        tv = sb("tv", [P, TB, HEADS, TOPK], f32, route)
        tci = sb("tci", [P, TB, HEADS, TOPK], u32, route)
        tab_u = sb("tab_u", [P, 2, TB, HEADS, TOPK], u32, route)
        tab_f = sb("tab_f", [P, 2, TB, HEADS, TOPK], f32, route)
        eq = [sb(f"eq{i}", [P, HEADS, TOPK, TOPK], f32, route) for i in range(2)]
        sel = sb("sel", [P, 3, TB, HEADS, TOPK], f32, route)
        ssum = sb("ssum", [P, TB, HEADS], f32, route)
        route.close()
        gates = sb("gates", [P, 2 * QUARTER, T], f32)
        ln2g = gates[:, 0:8, :].rearrange("p a b -> p (a b)")
        ln2b = gates[:, 8:16, :].rearrange("p a b -> p (a b)")

        bank = [ctx.enter_context(nc.psum_tensor(f"bank{i}", [P, DCH], f32)) for i in range(8)]

        y_banks = [[bank[6], bank[7]], [bank[4], bank[5]], [bank[1], bank[3]], [bank[0], bank[2]]]

        USED0, GLU0, S0, TAPS0, SC0 = 1, 2, 2, 1, 1

        raw_in = [sem(f"raw_in{i}") for i in range(RAW)]
        hi_done = sem("hi_done")
        lo_done = sem("lo_done")
        used = sem("used")
        xt_in = [sem(f"xt_in{i}") for i in range(4)]
        prm_in = sem("prm_in")
        xn_in = sem("xn_in")
        bo_in = sem("bo_in")
        xhi_done = sem("xhi_done")
        xlo_done = sem("xlo_done")
        pool_done = sem("pool_done")
        iota_done = sem("iota_done")
        sig_done = sem("sig_done")
        glu_done = sem("glu_done")
        taps_done = sem("taps_done")
        h_done = sem("h_done")
        sc_step = sem("sc_step")
        s_hi_done = sem("s_hi_done")
        s_done = sem("s_done")
        cconv_done = sem("cconv_done")
        mean_done = sem("mean_done")
        sq_done = sem("sq_done")
        cen_done = sem("cen_done")
        var_done = sem("var_done")
        veps_done = sem("veps_done")
        std_done = sem("std_done")
        cnorm_done = sem("cnorm_done")
        silu_done = sem("silu_done")
        a_hi_done = sem("a_hi_done")
        a_lo_done = sem("a_lo_done")
        xres_done = sem("xres_done")
        ln_chain = sem("ln_chain")
        ln_var = sem("ln_var")
        ln_std = sem("ln_std")
        ln1_in = sem("ln1_in")
        x1_done = sem("x1_done")
        x1_tr = sem("x1_tr")
        x1hi_done = sem("x1hi_done")
        x1lo_done = sem("x1lo_done")
        keys_in = sem("keys_in")
        qt_done = sem("qt_done")
        s_ready = sem("s_ready")
        rt = sem("rt")
        rt_exp_in = sem("rt_exp_in")
        rt_exp = sem("rt_exp")
        sel_done = sem("sel_done")
        sel_tr = sem("sel_tr")
        tabs_copied = sem("tabs_copied")
        tabs_done = sem("tabs_done")
        gelu_done = sem("gelu_done")
        oh_first = sem("oh_first")
        oh_chain = sem("oh_chain")
        oh_done = sem("oh_done")
        g_done = sem("g_done")
        gates_done = sem("gates_done")
        cf_done = sem("cf_done")
        chi_done = sem("chi_done")
        clo_done = sem("clo_done")
        acc_done = sem("acc_done")
        ln2_in = sem("ln2_in")
        fin = sem("fin")
        out_done = sem("out_done")

        block = ctx.enter_context(nc.Block())

        PER_HEAD = 2 * 11 + 2 + 12

        @block.sync
        def _(sp):
            def load(slot, src, u=None):
                if u is not None:
                    sp.wait_ge(lo_done, u - (RAW - 1))
                sp.dma_start(raw[:, slot, :], src).then_inc(raw_in[slot], 16)

            for c in range(4):
                sp.dma_start(xt_raw[:, 4 * c:4 * c + 4, :], x_t[:, 4 * c:4 * c + 4, :]).then_inc(xt_in[c], 16)
                for j in range(2):
                    load(2 * c + j, w_in[2 * c + j])
            sp.dma_start(acc[:, :, :], x_nat.rearrange("(b p) d -> p b d", p=P)).then_inc(xn_in, 16)
            sp.dma_start(bo[:, :], b_out.to_broadcast([P, D])).then_inc(bo_in, 16)
            sp.dma_start(keys[:, :], sub_keys).then_inc(keys_in, 16)
            for first, count, src in ((RAW, U_OUT, w_in), (0, U_Q - U_OUT, w_out)):
                base = 0 if src is w_in else U_OUT
                with sp.Fori(first // RAW, count // RAW) as i:
                    for s in range(RAW):
                        load(s, src[RAW * i + s], base + RAW * i + s)
            for dst, src in ((ln_g, ln1_g), (ln_b, ln1_b)):
                sp.dma_start(dst, src.to_broadcast([P, D])).then_inc(ln1_in, 16)
            with sp.Fori(0, (U_PRE - U_Q) // RAW) as i:
                for s in range(RAW):
                    load(s, w_q[RAW * i + s], U_Q + RAW * i + s)
            for r in range(2):
                for s in range(RAW):
                    load(s, u_w[RAW * r + s], U_PRE + RAW * r + s)
            with sp.Fori(0, (U_TAIL - U_MAIN) // RAW) as i:
                for s in range(RAW):
                    src = v_w[RAW // 2 * i + s // 4 * 2 + s % 2] if s % 4 < 2 else u_w[2 * RAW + RAW // 2 * i + s // 4 * 2 + s % 2]
                    load(s, src, U_MAIN + RAW * i + s)
            for r in range(2):
                for s in range(RAW):
                    load(s, v_w[(GROUPS - 2 + r) * RAW + s], U_TAIL + RAW * r + s)
            sp.wait_ge(cf_done, 24 * GROUP)
            for dst, src in ((ln2g, ln2_g), (ln2b, ln2_b)):
                sp.dma_start(dst, src.to_broadcast([P, D])).then_inc(ln2_in, 16)
            for b in range(TB):
                for h in range(2):
                    sp.wait_ge(fin, 2 * b + h + 1)
                    sp.dma_start(out[b * P:(b + 1) * P, h * D // 2:(h + 1) * D // 2],
                                 acc[:, b, h * D // 2:(h + 1) * D // 2]).then_inc(out_done, 16)
            sp.wait_ge(out_done, 64)

        @block.gpsimd
        def _(pool):
            nc.gpsimd.iota(iota[:, :], [[1, P]], base=0, channel_multiplier=0,
                           allow_small_or_imprecise_dtypes=True).then_inc(iota_done, 1)
            nc.gpsimd.memset(ident[:, :], 0.0).then_inc(pool_done, 1)
            nc.gpsimd.memset(ones[:, :], 1.0 / (CONF_TILES * P)).then_inc(pool_done, 1)
            nc.gpsimd.memset(apad[:, :, 0:TAPS - 1], 0.0).then_inc(pool_done, 1)
            nc.gpsimd.memset(scpad[:, 0:SC_TAPS - 1], 0.0).then_inc(pool_done, 1)
            pool.wait_ge(pool_done, 4)
            nc.gpsimd.affine_select(out=ident[:, :], in_=ident[:, :], compare_op=ALU.not_equal, fill=1.0,
                                    base=0, pattern=[[-1, P]], channel_multiplier=1).then_inc(pool_done, 1)

        @block.scalar
        def _(act):
            act.dma_start(prm[:, :], params).then_inc(prm_in, 16)

            def hi(u, slot_u):
                act.wait_ge(raw_in[slot_u % RAW], 16 // RAW * (u - slot_u % RAW) + 16)
                if not isinstance(u, int) or u >= SPLIT:
                    act.wait_ge(used, USED0 + u - (SPLIT - 1))
                nc.scalar.activation(w_hi[slot_u % SPLIT][:, :], raw[:, slot_u % RAW, :], ACT.Copy).then_inc(hi_done, 1)

            for c in range(4):
                act.wait_ge(xt_in[c], 16)
                nc.scalar.activation(xt_hi[:, 4 * c:4 * c + 4, :], xt_raw[:, 4 * c:4 * c + 4, :],
                                     ACT.Copy).then_inc(xhi_done, 1)
                if c < LEAD:
                    hi(c, c)
            act.wait_ge(prm_in, 16)
            with act.Fori(0, CONF_TILES // 2) as i:
                for b in range(2):
                    u = U_CONF + 8 * i + 4 * b + LEAD
                    t = 2 * i + b
                    for s in range(4):
                        hi(u + s, U_CONF + 4 * b + LEAD + s)
                    act.wait_ge(used, USED0 + u - LEAD + 4)
                    act.wait_ge(glu_done, GLU0 + t - 1)
                    nc.scalar.activation(sig[:, b, :], bank[2 + b][:, 0:T], ACT.Sigmoid,
                                         bias=prm[:, ds(PC_B + 2 * t + 1, 1)]).then_inc(sig_done, 1)
            with act.Fori(0, SC_TILES // 4) as i:
                for b in range(4):
                    u = U_SC + 24 * i + 6 * b + LEAD
                    t = 4 * i + b
                    for s in range(6):
                        hi(u + s, U_SC + 6 * b + LEAD + s)
                    act.wait_ge(used, USED0 + u - LEAD + 6)
                    act.wait_ge(s_done, S0 + t - 1)
                    nc.scalar.activation(hval[:, b % 2, :], bank[2 + b % 2][:, 0:T], ACT.Identity,
                                         bias=prm[:, ds(PC_B + 2 * CONF_TILES + 3 * t + 1, 1)]).then_inc(h_done, 1)
                    act.wait_ge(sc_step, 5 * t + 5)
                    nc.scalar.activation(mix_hi[:, ds(CONF_TILES + t, 1), :].rearrange("p a t -> p (a t)"), smix[:, :],
                                         ACT.Copy).then_inc(s_hi_done, 1)

            def stream_hi(first, n):
                for u in range(first, first + n):
                    hi(u, u)

            o = U_OUT + LEAD
            stream_hi(o, 4)
            act.wait_ge(cen_done, 1)
            nc.scalar.activation(cacc[:, 1, :, :], cacc[:, 0, :, :], ACT.Square).then_inc(sq_done, 1)
            stream_hi(o + 4, 4)
            act.wait_ge(veps_done, 1)
            nc.scalar.activation(lnt[:, 1, :], lnt[:, 0, :], ACT.Sqrt).then_inc(std_done, 1)
            stream_hi(o + 8, 1)
            act.wait_ge(cnorm_done, 1)
            for t in range(CONF_TILES):
                nc.scalar.activation(cacc[:, 1, t, :], cacc[:, 0, t, :], ACT.Silu, bias=prm[:, PC_LB + t:PC_LB + t + 1],
                                     scale=prm[:, PC_LG + t:PC_LG + t + 1]).then_inc(silu_done, 1)
            for h in range(2):
                act.wait_ge(silu_done, 4 * h + 4)
                nc.scalar.activation(mix_hi[:, 4 * h:4 * h + 4, :], cacc[:, 1, 4 * h:4 * h + 4, :],
                                     ACT.Copy).then_inc(a_hi_done, 1)
            stream_hi(o + 9, 32 - 9)
            for b in range(TB):
                act.wait_ge(ln_var, b + 1)
                nc.scalar.activation(rstd[:, b, :], mv[:, b, 1:2], ACT.Sqrt).then_inc(ln_std, 1)
            for n in range(8):
                b, k4 = n // 4, 4 * (n % 4)
                act.wait_ge(x1_tr, n + 1)
                nc.scalar.activation(xt_hi[:, k4:k4 + 4, b * P:(b + 1) * P],
                                     bank[n][:, :].rearrange("p (k t) -> p k t", t=P), ACT.Copy).then_inc(x1hi_done, 1)
            with act.Fori(0, HEADS // 2) as i:
                for b in range(4):
                    u = U_Q + 8 * i + 2 * b + LEAD
                    t = 4 * i + b
                    for s in range(2):
                        hi(u + s, U_Q + 2 * b + LEAD + s)
                    act.wait_ge(used, USED0 + u - LEAD + 2)
                    act.wait_ge(s_ready, SC0 + t)
                    nc.scalar.activation(q_t[b % 2][:, :], bank[b % 2][:, 0:T], ACT.Copy).then_inc(qt_done, 1)

            def gelu(c, c_ring, u_next):
                act.wait_ge(used, USED0 + u_next)
                if not isinstance(c, int) or c >= 2 * GROUP:
                    act.wait_ge(clo_done, c - 2 * GROUP + 1)
                nc.scalar.activation(stash[c_ring // GROUP % 2][:, c_ring % GROUP, :], bank[c_ring % 2][:, 0:T],
                                     ACT.Gelu).then_inc(gelu_done, 1)

            def gates_out(m, slot, t0, b):
                act.wait_ge(g_done, m + 1)
                nc.scalar.activation(gates[:, ds(slot, QUARTER), ds(t0, BATCH)].rearrange("p e t -> p t e"),
                                     bank[2 + b][:, 0:BATCH * QUARTER].rearrange("p (t e) -> p t e", e=QUARTER),
                                     ACT.Copy).then_inc(gates_done, 1)

            def coef_hi(c, c_ring):
                act.wait_ge(cf_done, c + 1)
                r, j = c_ring // GROUP % 2, c_ring % GROUP
                nc.scalar.activation(c_hi[r][:, j, :], stash[r][:, j, :], ACT.Copy).then_inc(chi_done, 1)

            for c in range(2 * GROUP):
                stream_hi(U_PRE + 2 * c + LEAD, 2)
                if c == 0:
                    act.wait_ge(rt_exp_in, 1)
                    nc.scalar.activation(sel[:, 2], sel[:, 2], ACT.Exp).then_inc(rt_exp, 1)
                gelu(c, c, U_PRE + 2 * c + 2)
            act.wait_ge(sel_tr, 1)
            nc.scalar.activation(gate_t[:, 0, :], bank[5][:, 0:T], ACT.Copy).then_inc(tabs_copied, 1)
            with act.Fori(0, T // BATCH // 2) as i:
                for b in range(2):
                    gates_out(2 * i + b, 0, 2 * BATCH * i + BATCH * b, b)
            with act.Fori(0, 2) as i:
                for b in range(2):
                    gates_out(T // BATCH + 2 * i + b, QUARTER, 2 * BATCH * i + BATCH * b, b)
            for c in range(GROUP):
                coef_hi(c, c)

            def group(g, par, ups, builds):
                for j in range(GROUP):
                    u = U_MAIN + GSTEP * g + STEP * j + LEAD if ups else U_TAIL + 2 * GROUP * (g - GROUPS + 2) + 2 * j + LEAD
                    ur = U_MAIN + STEP * j + LEAD + GSTEP * par if ups else U_TAIL + 2 * j + LEAD
                    n = STEP if ups else 2
                    for s in range(n):
                        if isinstance(u, int) and u + s >= U_END:
                            continue
                        hi(u + s, ur + s)
                        if s == 0 and not (isinstance(g, int) and g == GROUPS - 1):
                            coef_hi(GROUP * (g + 1) + j, GROUP * (par + 1) + j)
                    if ups:
                        gelu(GROUP * (g + 2) + j, GROUP * par + j, u - LEAD + STEP)
                    if builds:
                        m = GROUP * (g + 1) + j + T // BATCH
                        gates_out(m, QUARTER * (((g + 1) // GROUPS_Q + 1) % 2),
                                  BATCH * (GROUP * ((g + 1) % GROUPS_Q) + j), j % 2)

            group(0, 0, True, True)
            with act.Fori(0, 11) as p:
                for b in range(2):
                    group(2 * p + 1 + b, 1 + b, True, True)
            with act.Fori(11, 14) as p:
                for b in range(2):
                    group(2 * p + 1 + b, 1 + b, True, False)
            group(29, 1, True, False)
            group(30, 0, False, False)
            group(31, 1, False, False)
            for b in range(TB):
                act.wait_ge(ln_var, TB + b + 1)
                nc.scalar.activation(rstd[:, b, :], mv[:, b, 1:2], ACT.Sqrt).then_inc(ln_std, 1)

        @block.vector
        def _(dve):
            tt = nc.vector.tensor_tensor
            ts = nc.vector.tensor_scalar
            stt = nc.vector.scalar_tensor_tensor

            def lo(u, slot_u):
                dve.wait_ge(hi_done, u + 1)
                tt(w_lo[slot_u % SPLIT][:, :], raw[:, slot_u % RAW, :], w_hi[slot_u % SPLIT][:, :].bitcast(f32),
                   ALU.subtract).then_inc(lo_done, 1)

            def stream_lo(first, n):
                for u in range(first, first + n):
                    lo(u, u)

            for n, (credit, count) in enumerate(((used, USED0), (glu_done, GLU0), (s_done, S0), (taps_done, TAPS0), (s_ready, SC0))):
                nc.vector.memset(stats[:, 0, 0, n:n + 1], 0.0).then_inc(credit, count)
            for c in range(4):
                dve.wait_ge(xhi_done, c + 1)
                tt(xt_lo[:, 4 * c:4 * c + 4, :], xt_raw[:, 4 * c:4 * c + 4, :],
                   xt_hi[:, 4 * c:4 * c + 4, :].bitcast(f32), ALU.subtract).then_inc(xlo_done, 1)
                if c < LEAD:
                    lo(c, c)
            dve.wait_ge(prm_in, 16)
            dve.wait_ge(pool_done, 5)

            def tap(t, k, first_wait):
                a = apad[:, ds(t, 1), k:k + T]
                w = prm[:, ds(PC_CW + TAPS * t + k, 1)]
                s = cacc[:, k % 2, ds(t, 1), :]
                dve.wait_ge(taps_done, TAPS0 + first_wait)
                if k == 0:
                    i = ts(s, a, w, prm[:, ds(PC_CB + t, 1)], ALU.mult, ALU.add)
                elif k == 1:
                    i = ts(s, a, w, None, ALU.mult)
                else:
                    i = stt(s, a, w, s, ALU.mult, ALU.add)
                i.then_inc(taps_done, 1)

            def layer_norm(count, g, b_, done):
                n = [count]

                def link(ins):
                    n[0] += 1
                    ins.then_inc(ln_chain, 1)

                dve.wait_ge(ln_chain, n[0])
                for b in range(TB):
                    link(nc.vector.bn_aggr(mv[:, b, :], stats[:, b, :, :].rearrange("p c s -> p (c s)")))
                dve.wait_ge(ln_chain, n[0])
                for b in range(TB):
                    nc.vector.tensor_scalar_add(mv[:, b, 1:2], mv[:, b, 1:2], EPS).then_inc(ln_var, 1)
                base = TB if done is fin else 0
                for b in range(TB):
                    dve.wait_ge(ln_std, base + b + 1)
                    link(nc.vector.reciprocal(rstd[:, b, :], rstd[:, b, :]))
                half = D // 2
                for b in range(TB):
                    sl = [acc[:, b, h * half:(h + 1) * half] for h in range(2)]
                    dve.wait_ge(ln_chain, count + TB + b + 1 if b == 0 else n[0])
                    for h in range(2):
                        link(ts(sl[h], sl[h], mv[:, b, 0:1], rstd[:, b, :], ALU.subtract, ALU.mult))
                    for h in range(2):
                        dve.wait_ge(ln_chain, n[0] - 1)
                        link(tt(sl[h], sl[h], g[:, h * half:(h + 1) * half], ALU.mult))
                    for h in range(2):
                        dve.wait_ge(ln_chain, n[0] - 1 + h)
                        tt(sl[h], sl[h], b_[:, h * half:(h + 1) * half], ALU.add).then_inc(done, 1)

            H1 = 16
            with dve.Fori(0, CONF_TILES // 2) as i:
                for b in range(2):
                    u = U_CONF + 8 * i + 4 * b + LEAD
                    t = 2 * i + b
                    for s in range(4):
                        lo(u + s, U_CONF + 4 * b + LEAD + s)
                    dve.wait_ge(sig_done, t + 1)
                    stt(apad[:, ds(t, 1), TAPS - 1:TAPS - 1 + T].rearrange("p a t -> p (a t)"), bank[b][:, 0:T],
                        prm[:, ds(PC_B + 2 * t, 1)], sig[:, b, :], ALU.add, ALU.mult).then_inc(glu_done, 1)
                    dve.wait_ge(glu_done, GLU0 + t + 1)
                    for k in range(H1):
                        tap(t, k, H1 * t + max(k - 1, 0))
            dve.wait_ge(xn_in, 16)
            dve.wait_ge(bo_in, 16)
            for b in range(TB):
                stt(acc[:, b, :], acc[:, b, :], ALPHA, bo[:, :], ALU.mult, ALU.add).then_inc(xres_done, 1)
            T1 = H1 * CONF_TILES
            H2 = TAPS - H1
            with dve.Fori(0, SC_TILES // 4) as i:
                for b in range(4):
                    u = U_SC + 24 * i + 6 * b + LEAD
                    t = 4 * i + b
                    for s in range(6):
                        lo(u + s, U_SC + 6 * b + LEAD + s)
                    col = PC_B + 2 * CONF_TILES + 3 * t
                    ops = [
                        lambda: stt(scpad[:, 2:2 + T], bank[b % 2][:, 0:T], prm[:, ds(col, 1)], hval[:, b % 2, :],
                                    ALU.add, ALU.mult),
                        lambda: ts(sct[:, 0, :], scpad[:, 0:T], prm[:, ds(PC_SW + 3 * t, 1)],
                                   prm[:, ds(PC_SB + t, 1)], ALU.mult, ALU.add),
                        lambda: stt(sct[:, 1, :], scpad[:, 1:1 + T], prm[:, ds(PC_SW + 3 * t + 1, 1)], sct[:, 0, :],
                                    ALU.mult, ALU.add),
                        lambda: stt(sct[:, 0, :], scpad[:, 2:2 + T], prm[:, ds(PC_SW + 3 * t + 2, 1)], sct[:, 1, :],
                                    ALU.mult, ALU.add),
                        lambda: stt(smix[:, :], bank[4 + b % 2][:, 0:T], prm[:, ds(col + 2, 1)], sct[:, 0, :],
                                    ALU.add, ALU.mult),
                    ]
                    dve.wait_ge(h_done, t + 1)
                    for k in range(H2):
                        if k < len(ops):
                            if k:
                                dve.wait_ge(sc_step, 5 * t + k)
                            ops[k]().then_inc(sc_step, 1)
                        tap(t, H1 + k, T1 + H2 * t + max(k - 1, 0))
                    dve.wait_ge(s_hi_done, t + 1)
                    tt(mix_lo[:, ds(CONF_TILES + t, 1), :].rearrange("p a t -> p (a t)"), smix[:, :],
                       mix_hi[:, ds(CONF_TILES + t, 1), :].bitcast(f32).rearrange("p a t -> p (a t)"),
                       ALU.subtract).then_inc(s_done, 1)
            o = U_OUT + LEAD
            dve.wait_ge(taps_done, TAPS0 + T1 + H2 * CONF_TILES)
            tt(cacc[:, 0, :, :], cacc[:, 0, :, :], cacc[:, 1, :, :], ALU.add).then_inc(cconv_done, 1)
            stream_lo(o, 4)
            dve.wait_ge(mean_done, 1)
            tt(cacc[:, 0, :, :], cacc[:, 0, :, :], bank[0][:, 0:T].unsqueeze(1).to_broadcast([P, CONF_TILES, T]),
               ALU.subtract).then_inc(cen_done, 1)
            stream_lo(o + 4, 4)
            dve.wait_ge(var_done, 1)
            nc.vector.tensor_scalar_add(lnt[:, 0, :], bank[2][:, 0:T], EPS).then_inc(veps_done, 1)
            stream_lo(o + 8, 1)
            dve.wait_ge(std_done, 1)
            nc.vector.reciprocal(lnt[:, 0, :], lnt[:, 1, :]).then_inc(veps_done, 1)
            dve.wait_ge(veps_done, 2)
            tt(cacc[:, 0, :, :], cacc[:, 0, :, :], lnt[:, 0, :].unsqueeze(1).to_broadcast([P, CONF_TILES, T]),
               ALU.mult).then_inc(cnorm_done, 1)
            stream_lo_late = o + 9
            for h in range(2):
                dve.wait_ge(a_hi_done, h + 1)
                tt(mix_lo[:, 4 * h:4 * h + 4, :], cacc[:, 1, 4 * h:4 * h + 4, :],
                   mix_hi[:, 4 * h:4 * h + 4, :].bitcast(f32), ALU.subtract).then_inc(a_lo_done, 1)

            def add_y(b, d):
                sl = acc[:, b, d * DCH:(d + 1) * DCH]
                tt(sl, y_banks[d][b][:, :], sl, ALU.add).then_inc(ln_chain, 1)

            def bn(b, d, count):
                dve.wait_ge(ln_chain, count)
                nc.vector.bn_stats(stats[:, b, d, :], acc[:, b, d * DCH:(d + 1) * DCH]).then_inc(ln_chain, 1)

            stream_lo(stream_lo_late, 7)
            for d in range(3):
                stream_lo(o + 16 + 4 * d, 4)
                dve.wait_ge(used, USED0 + U_OUT + 16 + 4 * d)
                if d == 0:
                    dve.wait_ge(xres_done, 2)
                add_y(0, d)
                add_y(1, d)
                bn(0, d, 4 * d + 2)
                bn(1, d, 4 * d + 2)
            stream_lo(o + 28, 4)
            dve.wait_ge(used, USED0 + U_Q)
            add_y(0, 3)
            add_y(1, 3)
            bn(0, 3, 14)
            bn(1, 3, 14)
            dve.wait_ge(ln1_in, 32)
            layer_norm(4 * NCH, ln_g, ln_b, x1_done)
            for n in range(8):
                b, k4 = n // 4, 4 * (n % 4)
                dve.wait_ge(x1hi_done, n + 1)
                tt(xt_lo[:, k4:k4 + 4, b * P:(b + 1) * P], bank[n][:, :].rearrange("p (k t) -> p k t", t=P),
                   xt_hi[:, k4:k4 + 4, b * P:(b + 1) * P].bitcast(f32), ALU.subtract).then_inc(x1lo_done, 1)
            nc.vector.tensor_scalar_mul(acc[:, :, :], acc[:, :, :], ALPHA).then_inc(xres_done, 1)

            NEG = -3.0e38

            def top16(src, rest, v, idx, first):
                steps = [
                    lambda b: nc.vector.max(v(b, 0), src(b)),
                    lambda b: nc.vector.max_index(idx(b, 0), v(b, 0), src(b)),
                    lambda b: nc.vector.match_replace(rest(b), v(b, 0), src(b), NEG),
                    lambda b: nc.vector.max(v(b, 1), rest(b)),
                    lambda b: nc.vector.max_index(idx(b, 1), v(b, 1), rest(b)),
                ]
                needs = [None, 0, 0, 2, 3]
                for n, step in enumerate(steps):
                    for b in range(TB):
                        if needs[n] is not None:
                            dve.wait_ge(rt, first + 2 * needs[n] + b + 1)
                            dve.nop(nofuse=True)
                        step(b).then_inc(rt, 1)

            dve.wait_ge(iota_done, 1)
            dve.wait_ge(x1lo_done, 8)
            nc.vector.memset(ssum[:, :, :], 0.0).then_inc(rt, PER_HEAD)
            with dve.Fori(0, HEADS // 2) as i:
                for b4 in range(4):
                    u = U_Q + 8 * i + 2 * b4 + LEAD
                    t = 4 * i + b4
                    h = 2 * i + b4 // 2
                    r0 = PER_HEAD * (h + 1) + 11 * (b4 % 2)
                    for s in range(2):
                        lo(u + s, U_Q + 2 * b4 + LEAD + s)
                    dve.wait_ge(s_ready, SC0 + t + 1)
                    dve.nop(nofuse=True)
                    top16(lambda b: bank[2 + b4 % 2][:, b * P:(b + 1) * P],
                          lambda b: srest[:, b, :],
                          lambda b, e: hv[b4 % 2][:, b, 8 * e:8 * e + 8],
                          lambda b, e: hidx[b4 % 2][:, b, 8 * e:8 * e + 8], r0)
                    dve.wait_ge(rt, r0 + 10)
                    nc.vector.tensor_copy(hidx_f[:, :, ds(t, 1), :].rearrange("p b a k -> p b (a k)"),
                                          hidx[b4 % 2][:, :, :]).then_inc(rt, 1)
                    if b4 % 2:
                        r1 = PER_HEAD * (h + 1) + 22
                        dve.wait_ge(rt, r1)
                        for b in range(TB):
                            tt(cand[:, b, :, :],
                               hv[0][:, b, :].unsqueeze(2).to_broadcast([P, TOPK, TOPK]),
                               hv[1][:, b, :].unsqueeze(1).to_broadcast([P, TOPK, TOPK]), ALU.add).then_inc(rt, 1)
                        dve.wait_ge(rt, r1 + 2)
                        dve.nop(nofuse=True)
                        top16(lambda b: cand[:, b, :, :].rearrange("p a k -> p (a k)"),
                              lambda b: crest[:, b, :],
                              lambda b, e: cv[:, b, 8 * e:8 * e + 8],
                              lambda b, e: cidx[:, b, 8 * e:8 * e + 8], r1 + 2)
                        dve.wait_ge(rt, r1 + 12)
                        nc.vector.tensor_copy(tv[:, :, ds(h, 1), :].rearrange("p b a k -> p b (a k)"),
                                              cv[:, :, :]).then_inc(rt, 1)
                        nc.vector.tensor_copy(tci[:, :, ds(h, 1), :].rearrange("p b a k -> p b (a k)"),
                                              cidx[:, :, :]).then_inc(rt, 1)
            R = [PER_HEAD * (HEADS + 1)]

            def link(ins):
                R[0] += 1
                ins.then_inc(rt, 1)

            stream_lo(U_PRE + LEAD, 1)
            dve.wait_ge(rt, R[0])
            tt(sel[:, 2], tv[:, :, :, :], tv[:, :, :, 0:1].to_broadcast([P, TB, HEADS, TOPK]),
               ALU.subtract).then_inc(rt_exp_in, 1)
            link(nc.vector.tensor_single_scalar(tab_u[:, 0], tci[:, :, :, :], 4, ALU.logical_shift_right))
            link(nc.vector.tensor_single_scalar(tab_u[:, 1], tci[:, :, :, :], 15, ALU.bitwise_and))
            dve.wait_ge(rt, R[0])
            link(nc.vector.tensor_copy(tab_f[:, :, :, :, :], tab_u[:, :, :, :, :]))
            stream_lo(U_PRE + LEAD + 1, 1)
            dve.wait_ge(rt, R[0])
            n_eq = 0
            lo_next = U_PRE + LEAD + 2
            for half in range(2):
                for b in range(TB):
                    e = eq[n_eq % 2]
                    n_eq += 1
                    mine = hidx_f[:, b, :, :].rearrange("p (h two) k -> p h two k", two=2)[:, :, half, :]
                    link(tt(e[:, :, :, :], tab_f[:, half, b].unsqueeze(3).to_broadcast([P, HEADS, TOPK, TOPK]),
                            iota[:, 0:TOPK].unsqueeze(1).unsqueeze(1).to_broadcast([P, HEADS, TOPK, TOPK]),
                            ALU.is_equal))
                    stream_lo(lo_next, 1)
                    dve.wait_ge(rt, R[0])
                    link(tt(e[:, :, :, :], e[:, :, :, :], mine.unsqueeze(2).to_broadcast([P, HEADS, TOPK, TOPK]),
                            ALU.mult))
                    stream_lo(lo_next + 1, 1)
                    dve.wait_ge(rt, R[0])
                    link(nc.vector.tensor_reduce(sel[:, half, b], e[:, :, :, :], AX.X, ALU.add))
                    lo_next += 2
            dve.wait_ge(rt_exp, 1)
            link(nc.vector.tensor_reduce(ssum[:, :, :], sel[:, 2], AX.X, ALU.add))
            stream_lo(lo_next, 1)
            dve.wait_ge(rt, R[0])
            link(nc.vector.reciprocal(ssum[:, :, :], ssum[:, :, :]))
            stream_lo(lo_next + 1, 1)
            dve.wait_ge(rt, R[0])
            tt(sel[:, 2], sel[:, 2], ssum[:, :, :].unsqueeze(3).to_broadcast([P, TB, HEADS, TOPK]),
               ALU.mult).then_inc(sel_done, 1)
            lo_next += 2
            stream_lo(lo_next, U_MAIN + LEAD - lo_next)
            dve.wait_ge(sel_tr, 1)
            nc.vector.tensor_copy(tab1[:, :], bank[4][:, 0:T]).then_inc(tabs_done, 1)
            nc.vector.tensor_copy(tab2[:, :], bank[4][:, T:2 * T]).then_inc(tabs_done, 1)
            dve.wait_ge(tabs_copied, 1)
            tt(gate_t[:, 1, :], bank[5][:, 0:T], gate_t[:, 0, :].bitcast(f32), ALU.subtract).then_inc(tabs_done, 1)
            dve.wait_ge(tabs_done, 3)

            def onehot2(m, key0, t0):
                if not (isinstance(m, int) and m == 0):
                    dve.wait_ge(oh_chain, m)
                tt(oh2[:, :, :], iota[:, ds(key0, QUARTER)].unsqueeze(1).to_broadcast([P, BATCH, QUARTER]),
                   tab2[:, ds(t0, BATCH)].unsqueeze(2).to_broadcast([P, BATCH, QUARTER]), ALU.is_equal)\
                    .then_inc(oh_first, 1)

            def onehot1(m, t0, b):
                if not (isinstance(m, int) and m < 2):
                    dve.wait_ge(g_done, m - 1)
                tt(oh1[b][:, :, :], iota[:, :].unsqueeze(1).to_broadcast([P, BATCH, P]),
                   tab1[:, ds(t0, BATCH)].unsqueeze(2).to_broadcast([P, BATCH, P]), ALU.is_equal).then_inc(oh_done, 1)

            def gated(m, t0, b):
                dve.wait_ge(oh_first, m + 1)
                for part in range(2):
                    tt(oh2g[b][:, part, :, :], oh2[:, :, :],
                       gate_t[:, part, ds(t0, BATCH)].bitcast(f32).unsqueeze(2).to_broadcast([P, BATCH, QUARTER]),
                       ALU.mult).then_inc(oh_chain if part else oh_done, 1)

            def build(m, key0, t0, b):
                onehot2(m, key0, t0)
                onehot1(m, t0, b)
                gated(m, t0, b)

            build(0, 0, 0, 0)
            build(1, 0, BATCH, 1)
            with dve.Fori(1, T // BATCH // 2) as i:
                for b in range(2):
                    build(2 * i + b, 0, 2 * BATCH * i + BATCH * b, b)
            with dve.Fori(0, 2) as i:
                for b in range(2):
                    build(T // BATCH + 2 * i + b, QUARTER, 2 * BATCH * i + BATCH * b, b)

            def coef(c, c_ring, slot, gates_needed):
                dve.wait_ge(gelu_done, c + 1)
                dve.wait_ge(gates_done, gates_needed)
                s = stash[c_ring // GROUP % 2][:, c_ring % GROUP, :]
                tt(s, s, gates[:, ds(slot, 1), :].rearrange("p a t -> p (a t)"), ALU.mult).then_inc(cf_done, 1)

            def coef_lo(c, c_ring):
                dve.wait_ge(chi_done, c + 1)
                r, j = c_ring // GROUP % 2, c_ring % GROUP
                tt(c_lo[r][:, j, :], stash[r][:, j, :], c_hi[r][:, j, :].bitcast(f32), ALU.subtract).then_inc(clo_done, 1)

            dve.wait_ge(xres_done, 3)
            for c in range(GROUP):
                coef(c, c, c, T // BATCH)
            for c in range(GROUP):
                coef_lo(c, c)

            def add_v(u_next, c, b2):
                dve.wait_ge(used, USED0 + u_next)
                for b in range(TB):
                    sl = acc[:, b, c * DCH:(c + 1) * DCH]
                    i = tt(sl, bank[4 + 2 * (b2 % 2) + b][:, :], sl, ALU.add)
                i.then_inc(acc_done, 1)

            def group(g, par, ups, builds):
                more = not (isinstance(g, int) and g == GROUPS - 1)
                for j in range(GROUP):
                    u = U_MAIN + GSTEP * g + STEP * j + LEAD if ups else U_TAIL + 2 * GROUP * (g - GROUPS + 2) + 2 * j + LEAD
                    ur = U_MAIN + STEP * j + LEAD + GSTEP * par if ups else U_TAIL + 2 * j + LEAD
                    n = STEP if ups else 2
                    m = GROUP * (g + 1) + j + T // BATCH
                    t0 = BATCH * (GROUP * ((g + 1) % GROUPS_Q) + j)
                    for s in range(n):
                        if not (isinstance(u, int) and u + s >= U_END):
                            lo(u + s, ur + s)
                        if s == 0 and more:
                            c = GROUP * (g + 1) + j
                            coef(c, GROUP * (par + 1) + j, GROUP * ((g + 1) % (2 * GROUPS_Q)) + j,
                                 (T // BATCH) * ((g + 1) // GROUPS_Q + 1))
                            if builds:
                                onehot2(m, QUARTER * ((g + 1) // GROUPS_Q + 1), t0)
                        if s == 1 and more:
                            coef_lo(GROUP * (g + 1) + j, GROUP * (par + 1) + j)
                        if s == min(2, n - 1):
                            add_v(u - LEAD + 2, j, j)
                            if builds:
                                onehot1(m, t0, j % 2)
                    if builds:
                        gated(m, t0, j % 2)

            group(0, 0, True, True)
            with dve.Fori(0, 11) as p:
                for b in range(2):
                    group(2 * p + 1 + b, 1 + b, True, True)
            with dve.Fori(11, 14) as p:
                for b in range(2):
                    group(2 * p + 1 + b, 1 + b, True, False)
            group(29, 1, True, False)
            group(30, 0, False, False)
            group(31, 1, False, False)
            dve.wait_ge(acc_done, GROUPS * GROUP)
            for b in range(TB):
                for d in range(NCH):
                    nc.vector.bn_stats(stats[:, b, d, :], acc[:, b, d * DCH:(d + 1) * DCH]).then_inc(ln_chain, 1)
            dve.wait_ge(ln2_in, 32)
            layer_norm(4 * NCH + 2 * TB + 4 * TB + TB * NCH, ln2g, ln2b, fin)

        @block.tensor
        def _(pe):
            mm = nc.tensor.matmul

            def stationary_unit(u, slot_u, half, dst):
                pe.wait_ge(lo_done, u + 1)
                hi_w, lo_w = w_hi[slot_u % SPLIT], w_lo[slot_u % SPLIT]
                for k in range(HALF):
                    kk = HALF * half + k
                    sl = slice(k * P, (k + 1) * P)
                    st, en = half == 0 and k == 0, half == 1 and k == HALF - 1
                    mm(dst, hi_w[:, sl], xt_hi[:, kk, :], start=st, stop=False)
                    mm(dst, hi_w[:, sl], xt_lo[:, kk, :], start=False, stop=False)
                    i = mm(dst, lo_w[:, sl], xt_hi[:, kk, :], start=False, stop=en)
                i.then_inc(used, 1)

            for c in range(4):
                pe.wait_ge(xlo_done, c + 1)
            with pe.Fori(0, CONF_TILES // 2) as i:
                for b in range(2):
                    t = 2 * i + b
                    pe.wait_ge(glu_done, GLU0 + t - 1)
                    for w in range(2):
                        for h in range(2):
                            n = 4 * b + 2 * w + h
                            stationary_unit(U_CONF + 8 * i + n, U_CONF + n, h, bank[2 * w + b][:, 0:T])
            with pe.Fori(0, SC_TILES // 4) as i:
                for b in range(4):
                    t = 4 * i + b
                    if b < 2:
                        pe.wait_ge(glu_done, GLU0 + CONF_TILES)
                    pe.wait_ge(s_done, S0 + t - 1)
                    for w in range(3):
                        for h in range(2):
                            n = 6 * b + 2 * w + h
                            stationary_unit(U_SC + 24 * i + n, U_SC + n, h, bank[2 * w + b % 2][:, 0:T])

            def out_units(u0, k0, d, first, last):
                for n in range(4):
                    pe.wait_ge(lo_done, u0 + n + 1)
                    hi_w, lo_w = w_hi[(u0 + n) % SPLIT], w_lo[(u0 + n) % SPLIT]
                    for k in range(2):
                        kk = k0 + 2 * n + k
                        if u0 < U_OUT + 4:
                            pe.wait_ge(s_done, S0 + kk - CONF_TILES + 1)
                        st, en = first and n == 0 and k == 0, last and n == 3 and k == 1
                        w1, w2 = hi_w[:, k * DCH:(k + 1) * DCH], lo_w[:, k * DCH:(k + 1) * DCH]
                        for b in range(TB):
                            a1, a2 = mix_hi[:, kk, b * P:(b + 1) * P], mix_lo[:, kk, b * P:(b + 1) * P]
                            dst = y_banks[d][b][:, :]
                            mm(dst, a1, w1, start=st, stop=False)
                            mm(dst, a1, w2, start=False, stop=False)
                            i = mm(dst, a2, w1, start=False, stop=en)
                    i.then_inc(used, 1)

            out_units(U_OUT, CONF_TILES, 0, True, False)
            pe.wait_ge(cconv_done, 1)
            for t in range(CONF_TILES):
                i = mm(bank[0][:, 0:T], ones[:, :], cacc[:, 0, t, :], start=t == 0, stop=t == CONF_TILES - 1)
            i.then_inc(mean_done, 1)
            out_units(U_OUT + 4, CONF_TILES, 1, True, False)
            pe.wait_ge(sq_done, 1)
            for t in range(CONF_TILES):
                i = mm(bank[2][:, 0:T], ones[:, :], cacc[:, 1, t, :], start=t == 0, stop=t == CONF_TILES - 1)
            i.then_inc(var_done, 1)
            out_units(U_OUT + 8, CONF_TILES, 2, True, False)
            pe.wait_ge(a_lo_done, 2)
            for d in range(3):
                out_units(U_OUT + 12 + 4 * d, 0, d, False, True)
            pe.wait_ge(veps_done, 1)
            out_units(U_OUT + 24, CONF_TILES, 3, True, False)
            out_units(U_OUT + 28, 0, 3, False, True)
            pe.wait_ge(pool_done, 5)
            for n in range(8):
                b, k4 = n // 4, 4 * (n % 4)
                pe.wait_ge(x1_done, 2 * b + (n % 4) // 2 + 1)
                for k in range(4):
                    i = nc.tensor.transpose(bank[n][:, k * P:(k + 1) * P], acc[:, b, (k4 + k) * P:(k4 + k + 1) * P],
                                            ident[:, :])
                i.then_inc(x1_tr, 1)
            pe.wait_ge(x1lo_done, 8)
            pe.wait_ge(keys_in, 16)

            def scores(t, b4, h_pair):
                pe.wait_ge(qt_done, t + 1)
                pe.wait_ge(rt, PER_HEAD * (2 * h_pair + b4 // 2) + 11 * (b4 % 2) + 6)
                for b in range(TB):
                    i = mm(bank[2 + b4 % 2][:, b * P:(b + 1) * P], q_t[b4 % 2][:, b * P:(b + 1) * P],
                           keys[:, ds(N_KEYS * t, N_KEYS)], start=True, stop=True)
                i.then_inc(s_ready, 1)

            with pe.Fori(0, HEADS // 2) as i:
                for b4 in range(4):
                    t = 4 * i + b4
                    n = 2 * b4
                    stationary_unit(U_Q + 8 * i + n, U_Q + n, 0, bank[b4 % 2][:, 0:T])
                    if b4:
                        scores(t - 1, b4 - 1, i)
                    stationary_unit(U_Q + 8 * i + n + 1, U_Q + n + 1, 1, bank[b4 % 2][:, 0:T])
                scores(4 * i + 3, 3, i)

            def up(c, c_ring, u, ur, free):
                if free:
                    pe.wait_ge(gelu_done, c - 1)
                for h in range(2):
                    stationary_unit(u + h, ur + h, h, bank[c_ring % 2][:, 0:T])

            for c in range(2 * GROUP):
                up(c, c, U_PRE + 2 * c, U_PRE + 2 * c, c >= 2)

            pe.wait_ge(sel_done, 1)
            for w in range(3):
                dst = bank[4 + w // 2]
                for b in range(TB):
                    i = nc.tensor.transpose(dst[:, (w % 2) * T + b * P:(w % 2) * T + (b + 1) * P],
                                            sel[:, w, b].rearrange("p h k -> p (h k)"), ident[:, :])
            i.then_inc(sel_tr, 1)

            def gate_batch(m, b, first):
                pe.wait_ge(oh_chain, m + 1)
                pe.wait_ge(oh_done, 2 * m + 2)
                if not first:
                    pe.wait_ge(gates_done, m - 1)
                for t in range(BATCH):
                    dst = bank[2 + b][:, t * QUARTER:(t + 1) * QUARTER]
                    mm(dst, oh1[b][:, t, :], oh2g[b][:, 0, t, :], start=True, stop=False)
                    i = mm(dst, oh1[b][:, t, :], oh2g[b][:, 1, t, :], start=False, stop=True)
                i.then_inc(g_done, 1)

            gate_batch(0, 0, True)
            gate_batch(1, 1, True)
            with pe.Fori(1, (T + GROUP * BATCH) // BATCH // 2) as i:
                for b in range(2):
                    gate_batch(2 * i + b, b, False)

            def down(n, par, j, u, ur, free):
                if free:
                    pe.wait_ge(acc_done, n - 1)
                for h in range(2):
                    pe.wait_ge(lo_done, u + h + 1)
                    hi_w, lo_w = w_hi[(ur + h) % SPLIT], w_lo[(ur + h) % SPLIT]
                    for e in range(2):
                        w1, w2 = hi_w[:, e * DCH:(e + 1) * DCH], lo_w[:, e * DCH:(e + 1) * DCH]
                        for b in range(TB):
                            dst = bank[4 + 2 * (j % 2) + b][:, :]
                            a1 = c_hi[par][:, 2 * h + e, b * P:(b + 1) * P]
                            a2 = c_lo[par][:, 2 * h + e, b * P:(b + 1) * P]
                            mm(dst, a1, w1, start=h == 0 and e == 0, stop=False)
                            mm(dst, a1, w2, start=False, stop=False)
                            i = mm(dst, a2, w1, start=False, stop=h == 1 and e == 1)
                    i.then_inc(used, 1)

            def group(g, par, ups, builds):
                first = isinstance(g, int) and g == 0
                for j in range(GROUP):
                    u = U_MAIN + GSTEP * g + STEP * j if ups else U_TAIL + 2 * GROUP * (g - GROUPS + 2) + 2 * j
                    ur = U_MAIN + STEP * j if ups else U_TAIL + 2 * j
                    if j == 0:
                        pe.wait_ge(clo_done, GROUP * (g + 1))
                    down(GROUP * g + j, par % 2, j, u, ur, not (first and j < 2))
                    if ups:
                        up(GROUP * (g + 2) + j, GROUP * par + j, u + 2, ur + 2, True)
                    if builds:
                        gate_batch(GROUP * (g + 1) + j + T // BATCH, j % 2, False)

            group(0, 0, True, True)
            with pe.Fori(0, 11) as p:
                for b in range(2):
                    group(2 * p + 1 + b, 1 + b, True, True)
            with pe.Fori(11, 14) as p:
                for b in range(2):
                    group(2 * p + 1 + b, 1 + b, True, False)
            group(29, 1, True, False)
            group(30, 0, False, False)
            group(31, 1, False, False)


_OUT_SHAPE = (1, T, D)


def kernel(**inputs):
    import numpy as _np
    import concourse.bacc as _bacc
    from concourse import mybir as _mybir
    from concourse.bass_utils import run_bass_kernel_spmd as _run

    a = {name: _np.asarray(value) for name, value in inputs.items()}
    c, s = CONF_TILES, SC_TILES
    order = [t for i in range(c) for t in (i, c + i)] + [2 * c + t for i in range(s) for t in (s + i, 2 * s + i, i)]

    def stationary_units(w):
        n = w.shape[1] // P
        return w.reshape(2, HALF, P, n, P).transpose(3, 0, 2, 1, 4)

    w_in = stationary_units(a["w_in"][0])[order]
    w_q = stationary_units(a["w_q"][0])
    u_w = a["peer_u"][0].reshape(N_KEYS, N_KEYS, 2, HALF, P).transpose(1, 2, 4, 3, 0)
    v_w = a["peer_v"][0].reshape(N_KEYS, GROUPS, 2, 2, NCH, DCH).transpose(1, 4, 2, 0, 3, 5)
    w_out = a["w_out"][0].reshape(2, 4, 2, P, NCH, DCH).transpose(4, 0, 1, 3, 2, 5)
    w_out = _np.concatenate([w_out[0:3, 1], w_out[0:3, 0], w_out[3:4, 1], w_out[3:4, 0]])
    cols = [a["b_in"][0].reshape(-1, P)[order].T,
            a["conf_conv_w"][0].reshape(TAPS, c, P).transpose(2, 1, 0).reshape(P, -1),
            a["conf_conv_b"][0].reshape(c, P).T, a["conf_ln_g"][0].reshape(c, P).T, a["conf_ln_b"][0].reshape(c, P).T,
            a["sc_conv_w"][0].reshape(SC_TAPS, s, P).transpose(2, 1, 0).reshape(P, -1),
            a["sc_conv_b"][0].reshape(s, P).T]
    laid = {
        "x_t": a["x"][0].reshape(T, KT, P).transpose(2, 1, 0),
        "x_nat": a["x"][0],
        "w_in": w_in.reshape(-1, P, HALF * P),
        "w_out": w_out.reshape(-1, P, HALF * P),
        "w_q": w_q.reshape(-1, P, HALF * P),
        "u_w": u_w.reshape(-1, P, HALF * P),
        "v_w": v_w.reshape(-1, P, HALF * P),
        "params": _np.concatenate(cols, axis=1),
        "sub_keys": a["sub_keys"][0].transpose(3, 0, 1, 2).reshape(P, -1),
    }
    for name in ("b_out", "ln1_g", "ln1_b", "ln2_g", "ln2_b"):
        laid[name] = a[name].reshape(1, D)

    nc = _bacc.Bacc("TRN2", target_bir_lowering=False, num_devices=1, dynamic_dma_scratch_size=1024)
    arrays, args = {}, []
    for name, value in laid.items():
        value = _np.ascontiguousarray(value)
        arrays[f"in_{name}_dram"] = value
        args.append(nc.dram_tensor(f"in_{name}_dram", value.shape, _mybir.dt.from_np(value.dtype),
                                   kind="ExternalInput").ap())
    args.append(nc.dram_tensor("out_dram", _OUT_SHAPE[1:], _mybir.dt.float32, kind="ExternalOutput").ap())
    build(nc, *args)
    r = _run(nc, [arrays], core_ids=[0])
    return r.results[0]["out_dram"].reshape(_OUT_SHAPE)
```

```python
import concourse.bass as bass
from concourse import mybir
from contextlib import ExitStack

P = 128
T = 256
TB = T // P
D = 2048
KT = D // P
HALF = KT // 2
CONF_TILES = 8
SC_TILES = 8
TAPS = 31
SC_TAPS = 3
HEADS = 8
TOPK = 16
N_KEYS = 128
DCH = 512
NCH = D // DCH
GROUP = 4
GROUPS = N_KEYS // GROUP
QUARTER = 32
GROUPS_Q = QUARTER // GROUP
BATCH = 8
ALPHA = 2.0 ** 0.25
EPS = 1e-5
RAW = 4
SPLIT = 4
LEAD = 3
HLEAD = LEAD + 1
AHEAD = 6
UP_FIRST = 10
UP_LOOPS = 7

U_CONF = 0
U_SC = U_CONF + 2 * 2 * CONF_TILES
U_OUT = U_SC + 3 * 2 * SC_TILES
U_Q = U_OUT + NCH * HALF
U_PRE = U_Q + 2 * 2 * HEADS
U_MAIN = U_PRE + AHEAD * GROUP * 2
STEP = 4
GSTEP = GROUP * STEP
U_TAIL = U_MAIN + (GROUPS - AHEAD) * GSTEP
U_END = U_TAIL + AHEAD * 2 * GROUP
PC_B = 0
PC_CW = PC_B + 2 * CONF_TILES + 3 * SC_TILES
PC_CB = PC_CW + CONF_TILES * TAPS
PC_LG = PC_CB + CONF_TILES
PC_LB = PC_LG + CONF_TILES
PC_SW = PC_LB + CONF_TILES
PC_SB = PC_SW + SC_TILES * SC_TAPS
PC_END = PC_SB + SC_TILES


def build(nc, x_t, x_nat, w_in, w_out, w_q, u_w, v_w, params, sub_keys, b_out, ln1_g, ln1_b, ln2_g, ln2_b, out):
    f32 = mybir.dt.float32
    f32r = mybir.dt.float32r
    u32 = mybir.dt.uint32
    ALU = mybir.AluOpType
    ACT = mybir.ActivationFunctionType
    AX = mybir.AxisListType
    ds = bass.ds

    ctx = ExitStack()
    with ctx:
        def sb(name, shape, dt, where=ctx):
            return where.enter_context(nc.sbuf_tensor(name, shape, dt))

        def sem(name):
            return ctx.enter_context(nc.semaphore(name))

        raw = sb("raw", [P, RAW, HALF * P], f32)
        w_hi = [sb(f"w_hi{i}", [P, HALF * P], f32r) for i in range(SPLIT)]
        w_lo = [sb(f"w_lo{i}", [P, HALF * P], f32r) for i in range(SPLIT)]
        xt_hi = sb("xt_hi", [P, KT, T], f32r)
        xt_lo = sb("xt_lo", [P, KT, T], f32r)
        acc = sb("acc", [P, TB, D], f32)
        iota = sb("iota", [P, P], f32)
        ident = sb("ident", [P, P], f32)
        stats = sb("stats", [P, TB, NCH, 6], f32)
        mv = sb("mv", [P, TB, 2], f32)
        rstd = sb("rstd", [P, TB, 1], f32)
        early = ExitStack()
        keys = sb("keys", [P, 2 * HEADS * N_KEYS], f32, early)
        xt_raw = sb("xt_raw", [P, KT, T], f32, early)
        prm = sb("prm", [P, PC_END], f32, early)
        apad = sb("apad", [P, CONF_TILES, TAPS - 1 + T], f32, early)
        cacc = sb("cacc", [P, 2, CONF_TILES, T], f32, early)
        mix_hi = sb("mix_hi", [P, KT, T], f32r, early)
        mix_lo = sb("mix_lo", [P, KT, T], f32r, early)
        scpad = sb("scpad", [P, SC_TAPS - 1 + T], f32, early)
        sct = sb("sct", [P, 2, T], f32, early)
        sig = sb("sig", [P, 2, T], f32, early)
        hval = sb("hval", [P, 2, T], f32, early)
        smix = sb("smix", [P, T], f32, early)
        ones = sb("ones", [P, P], f32, early)
        lnt = sb("lnt", [P, 2, T], f32, early)
        ln_g = xt_raw[:, 0:8, :].rearrange("p a b -> p (a b)")
        ln_b = xt_raw[:, 8:16, :].rearrange("p a b -> p (a b)")
        bo = sb("bo", [P, D], f32, early)
        early.close()
        c_hi = [sb(f"c_hi{i}", [P, GROUP, T], f32r) for i in range(2)]
        c_lo = [sb(f"c_lo{i}", [P, GROUP, T], f32r) for i in range(2)]
        tab1 = sb("tab1", [P, T], f32)
        tab2 = sb("tab2", [P, T], f32)
        gate_t = sb("gate_t", [P, 2, T], f32r)
        stash = sb("stash", [P, AHEAD * GROUP, T], f32)
        oh1 = [sb(f"oh1_{i}", [P, BATCH, P], f32r) for i in range(2)]
        oh2 = sb("oh2", [P, BATCH, QUARTER], f32)
        oh2g = [sb(f"oh2g_{i}", [P, BATCH, 2, QUARTER], f32r) for i in range(2)]
        route = ExitStack()
        q_t = [sb(f"q_t{i}", [P, T], f32, route) for i in range(2)]
        srest = sb("srest", [P, TB, N_KEYS], f32, route)
        cand = sb("cand", [P, TB, TOPK, TOPK], f32, route)
        crest = sb("crest", [P, TB, TOPK * TOPK], f32, route)
        hv = [sb(f"hv{i}", [P, TB, TOPK], f32, route) for i in range(2)]
        hidx = [sb(f"hidx{i}", [P, TB, TOPK], u32, route) for i in range(2)]
        cv = sb("cv", [P, TB, TOPK], f32, route)
        cidx = sb("cidx", [P, TB, TOPK], u32, route)
        hidx_f = sb("hidx_f", [P, TB, 2 * HEADS, TOPK], f32, route)
        tv = sb("tv", [P, TB, HEADS, TOPK], f32, route)
        tci = sb("tci", [P, TB, HEADS, TOPK], u32, route)
        tab_u = sb("tab_u", [P, 2, TB, HEADS, TOPK], u32, route)
        tab_f = sb("tab_f", [P, 2, TB, HEADS, TOPK], f32, route)
        eq = [sb(f"eq{i}", [P, HEADS, TOPK, TOPK], f32, route) for i in range(2)]
        sel = sb("sel", [P, 3, TB, HEADS, TOPK], f32, route)
        ssum = sb("ssum", [P, TB, HEADS], f32, route)
        route.close()
        gates = sb("gates", [P, 2 * QUARTER, T], f32)
        ln2g = gates[:, 0:8, :].rearrange("p a b -> p (a b)")
        ln2b = gates[:, 8:16, :].rearrange("p a b -> p (a b)")

        bank = [ctx.enter_context(nc.psum_tensor(f"bank{i}", [P, DCH], f32)) for i in range(8)]

        y_banks = [[bank[6], bank[7]], [bank[4], bank[5]], [bank[1], bank[3]], [bank[0], bank[2]]]

        USED0, GLU0, S0, TAPS0, SC0, GATES0 = 1, 2, 2, 1, 1, 2

        raw_in = [sem(f"raw_in{i}") for i in range(RAW)]
        hi_done = sem("hi_done")
        lo_even = sem("lo_even")
        lo_odd = sem("lo_odd")
        used = sem("used")
        xt_in = [sem(f"xt_in{i}") for i in range(4)]
        prm_in = sem("prm_in")
        xn_in = sem("xn_in")
        bo_in = sem("bo_in")
        xhi_done = sem("xhi_done")
        xlo_done = sem("xlo_done")
        pool_done = sem("pool_done")
        iota_done = sem("iota_done")
        sig_done = sem("sig_done")
        glu_done = sem("glu_done")
        taps_done = sem("taps_done")
        h_done = sem("h_done")
        sc_step = sem("sc_step")
        s_hi_done = sem("s_hi_done")
        s_done = sem("s_done")
        cconv_done = sem("cconv_done")
        mean_done = sem("mean_done")
        sq_done = sem("sq_done")
        cen_done = sem("cen_done")
        var_done = sem("var_done")
        veps_done = sem("veps_done")
        std_done = sem("std_done")
        cnorm_done = sem("cnorm_done")
        silu_done = sem("silu_done")
        a_hi_done = sem("a_hi_done")
        a_lo_done = sem("a_lo_done")
        xres_done = sem("xres_done")
        ln_chain = sem("ln_chain")
        ln_var = sem("ln_var")
        ln_std = sem("ln_std")
        ln1_in = sem("ln1_in")
        x1_done = sem("x1_done")
        x1_tr = sem("x1_tr")
        x1hi_done = sem("x1hi_done")
        x1lo_done = sem("x1lo_done")
        keys_in = sem("keys_in")
        qt_done = sem("qt_done")
        s_ready = sem("s_ready")
        rt = sem("rt")
        rt_exp_in = sem("rt_exp_in")
        rt_exp = sem("rt_exp")
        sel_done = sem("sel_done")
        sel_tr = sem("sel_tr")
        tabs_copied = sem("tabs_copied")
        tabs_done = sem("tabs_done")
        gelu_done = sem("gelu_done")
        oh_first = sem("oh_first")
        oh_chain = sem("oh_chain")
        oh_done = sem("oh_done")
        g_done = sem("g_done")
        gates_up = sem("gates_up")
        gates_done = sem("gates_done")
        cf_done = sem("cf_done")
        chi_done = sem("chi_done")
        clo_done = sem("clo_done")
        acc_done = sem("acc_done")
        ln2_in = sem("ln2_in")
        fin = sem("fin")
        out_done = sem("out_done")

        block = ctx.enter_context(nc.Block())

        PER_HEAD = 2 * 11 + 2 + 12

        def wait_lo(engine, u, slot_u):
            engine.wait_ge(lo_odd if slot_u % 2 else lo_even, u + (1 if slot_u % 2 else 2))

        @block.sync
        def _(sp):
            def load(slot, src, u=None):
                if u is not None:
                    wait_lo(sp, u - RAW, slot)
                sp.dma_start(raw[:, slot, :], src).then_inc(raw_in[slot], 16)

            def load_x(c):
                sp.dma_start(xt_raw[:, 4 * c:4 * c + 4, :], x_t[:, 4 * c:4 * c + 4, :]).then_inc(xt_in[c], 16)

            load(0, w_in[0])
            load_x(0)
            load_x(1)
            load(1, w_in[1])
            load_x(2)
            load_x(3)
            load(2, w_in[2])
            load(3, w_in[3])
            sp.dma_start(acc[:, :, :], x_nat.rearrange("(b p) d -> p b d", p=P)).then_inc(xn_in, 16)
            sp.dma_start(bo[:, :], b_out.to_broadcast([P, D])).then_inc(bo_in, 16)
            sp.dma_start(keys[:, :], sub_keys).then_inc(keys_in, 16)
            for first, count, src in ((RAW, U_OUT, w_in), (0, U_Q - U_OUT, w_out)):
                base = 0 if src is w_in else U_OUT
                with sp.Fori(first // RAW, count // RAW) as i:
                    for s in range(RAW):
                        load(s, src[RAW * i + s], base + RAW * i + s)
            for dst, src in ((ln_g, ln1_g), (ln_b, ln1_b)):
                sp.dma_start(dst, src.to_broadcast([P, D])).then_inc(ln1_in, 16)
            with sp.Fori(0, (U_PRE - U_Q) // RAW) as i:
                for s in range(RAW):
                    load(s, w_q[RAW * i + s], U_Q + RAW * i + s)
            with sp.Fori(0, (U_MAIN - U_PRE) // RAW) as i:
                for s in range(RAW):
                    load(s, u_w[RAW * i + s], U_PRE + RAW * i + s)
            with sp.Fori(0, (U_TAIL - U_MAIN) // STEP) as i:
                for s in range(STEP):
                    load(s, v_w[2 * i + s] if s < 2 else u_w[2 * AHEAD * GROUP + 2 * i + s - 2],
                         U_MAIN + STEP * i + s)
            with sp.Fori(0, (U_END - U_TAIL) // RAW) as i:
                for s in range(RAW):
                    load(s, v_w[2 * GROUP * (GROUPS - AHEAD) + RAW * i + s], U_TAIL + RAW * i + s)
            sp.wait_ge(cf_done, 24 * GROUP)
            for dst, src in ((ln2g, ln2_g), (ln2b, ln2_b)):
                sp.dma_start(dst, src.to_broadcast([P, D])).then_inc(ln2_in, 16)
            for d in range(NCH):
                for b in range(TB):
                    sp.wait_ge(fin, TB * d + b + 1)
                    sp.dma_start(out[b * P:(b + 1) * P, d * DCH:(d + 1) * DCH],
                                 acc[:, b, d * DCH:(d + 1) * DCH]).then_inc(out_done, 16)
            sp.wait_ge(out_done, 16 * NCH * TB)

        @block.gpsimd
        def _(pool):
            nc.gpsimd.iota(iota[:, :], [[1, P]], base=0, channel_multiplier=0,
                           allow_small_or_imprecise_dtypes=True).then_inc(iota_done, 1)
            nc.gpsimd.memset(ident[:, :], 0.0).then_inc(pool_done, 1)
            nc.gpsimd.memset(ones[:, :], 1.0 / (CONF_TILES * P)).then_inc(pool_done, 1)
            nc.gpsimd.memset(apad[:, :, 0:TAPS - 1], 0.0).then_inc(pool_done, 1)
            nc.gpsimd.memset(scpad[:, 0:SC_TAPS - 1], 0.0).then_inc(pool_done, 1)
            pool.wait_ge(pool_done, 4)
            nc.gpsimd.affine_select(out=ident[:, :], in_=ident[:, :], compare_op=ALU.not_equal, fill=1.0,
                                    base=0, pattern=[[-1, P]], channel_multiplier=1).then_inc(pool_done, 1)
            with pool.Fori(0, U_END // RAW) as i:
                for s in range(1, RAW, 2):
                    pool.wait_ge(hi_done, RAW * i + s + 1)
                    nc.gpsimd.tensor_tensor(w_lo[s][:, :], raw[:, s, :], w_hi[s][:, :].bitcast(f32),
                                            ALU.subtract).then_inc(lo_odd, 2)

        @block.scalar
        def _(act):
            act.dma_start(prm[:, :], params).then_inc(prm_in, 16)

            def hi(u, slot_u):
                act.wait_ge(raw_in[slot_u % RAW], 16 // RAW * (u - slot_u % RAW) + 16)
                if not isinstance(u, int) or u >= SPLIT:
                    act.wait_ge(used, USED0 + u - (SPLIT - 1))
                nc.scalar.activation(w_hi[slot_u % SPLIT][:, :], raw[:, slot_u % RAW, :], ACT.Copy).then_inc(hi_done, 1)

            def x_hi(c):
                act.wait_ge(xt_in[c], 16)
                nc.scalar.activation(xt_hi[:, 4 * c:4 * c + 4, :], xt_raw[:, 4 * c:4 * c + 4, :],
                                     ACT.Copy).then_inc(xhi_done, 1)

            hi(0, 0)
            x_hi(0)
            x_hi(1)
            hi(1, 1)
            x_hi(2)
            x_hi(3)
            hi(2, 2)
            hi(3, 3)
            act.wait_ge(prm_in, 16)
            with act.Fori(0, CONF_TILES // 2) as i:
                for b in range(2):
                    u = U_CONF + 8 * i + 4 * b
                    t = 2 * i + b
                    for s in range(3):
                        hi(u + HLEAD + s, U_CONF + 4 * b + HLEAD + s)
                    act.wait_ge(used, USED0 + u + 4)
                    act.wait_ge(glu_done, GLU0 + t - 1)
                    nc.scalar.activation(sig[:, b, :], bank[2 + b][:, 0:T], ACT.Sigmoid,
                                         bias=prm[:, ds(PC_B + 2 * t + 1, 1)]).then_inc(sig_done, 1)
                    hi(u + HLEAD + 3, U_CONF + 4 * b + HLEAD + 3)
            for s in range(2):
                hi(U_SC + HLEAD + s, U_SC + HLEAD + s)
            with act.Fori(0, SC_TILES // 4) as i:
                for b in range(4):
                    u = U_SC + 24 * i + 6 * b
                    t = 4 * i + b
                    for s in range(2, 5):
                        hi(u + HLEAD + s, U_SC + 6 * b + HLEAD + s)
                    act.wait_ge(used, USED0 + u + 6)
                    act.wait_ge(s_done, S0 + t - 1)
                    nc.scalar.activation(hval[:, b % 2, :], bank[2 + b % 2][:, 0:T], ACT.Identity,
                                         bias=prm[:, ds(PC_B + 2 * CONF_TILES + 3 * t + 1, 1)]).then_inc(h_done, 1)
                    for s in range(5, 8):
                        hi(u + HLEAD + s, U_SC + 6 * b + HLEAD + s)
                    act.wait_ge(sc_step, 5 * t + 5)
                    nc.scalar.activation(mix_hi[:, ds(CONF_TILES + t, 1), :].rearrange("p a t -> p (a t)"), smix[:, :],
                                         ACT.Copy).then_inc(s_hi_done, 1)

            def stream_hi(first, n):
                for u in range(first, first + n):
                    hi(u, u)

            o = U_OUT + HLEAD
            stream_hi(o + 2, 7)
            act.wait_ge(cen_done, 1)
            nc.scalar.activation(cacc[:, 1, :, :], cacc[:, 0, :, :], ACT.Square).then_inc(sq_done, 1)
            stream_hi(o + 9, 3)
            act.wait_ge(veps_done, 1)
            nc.scalar.activation(lnt[:, 1, :], lnt[:, 0, :], ACT.Sqrt).then_inc(std_done, 1)
            stream_hi(o + 12, 1)
            act.wait_ge(cnorm_done, 1)
            for t in range(CONF_TILES):
                nc.scalar.activation(cacc[:, 1, t, :], cacc[:, 0, t, :], ACT.Silu, bias=prm[:, PC_LB + t:PC_LB + t + 1],
                                     scale=prm[:, PC_LG + t:PC_LG + t + 1]).then_inc(silu_done, 1)
            for h in range(2):
                act.wait_ge(silu_done, 4 * h + 4)
                nc.scalar.activation(mix_hi[:, 4 * h:4 * h + 4, :], cacc[:, 1, 4 * h:4 * h + 4, :],
                                     ACT.Copy).then_inc(a_hi_done, 1)
            stream_hi(o + 13, 19)
            for b in range(TB):
                act.wait_ge(ln_var, b + 1)
                nc.scalar.activation(rstd[:, b, :], mv[:, b, 1:2], ACT.Sqrt).then_inc(ln_std, 1)
            for n in range(8):
                k4, b = 4 * (n // TB), n % TB
                act.wait_ge(x1_tr, n + 1)
                nc.scalar.activation(xt_hi[:, k4:k4 + 4, b * P:(b + 1) * P],
                                     bank[n][:, :].rearrange("p (k t) -> p k t", t=P), ACT.Copy).then_inc(x1hi_done, 1)
            with act.Fori(0, HEADS // 2) as i:
                for b in range(4):
                    u = U_Q + 8 * i + 2 * b
                    t = 4 * i + b
                    hi(u + HLEAD, U_Q + 2 * b + HLEAD)
                    act.wait_ge(used, USED0 + u + 2)
                    act.wait_ge(s_ready, SC0 + t)
                    nc.scalar.activation(q_t[b % 2][:, :], bank[b % 2][:, 0:T], ACT.Copy).then_inc(qt_done, 1)
                    hi(u + HLEAD + 1, U_Q + 2 * b + HLEAD + 1)

            def gelu(c, bank_no, u_next, again=True):
                act.wait_ge(used, USED0 + u_next)
                if again:
                    act.wait_ge(clo_done, c - AHEAD * GROUP + 1)
                nc.scalar.activation(stash[:, ds(c % (AHEAD * GROUP), 1), :].rearrange("p a t -> p (a t)"),
                                     bank[bank_no][:, 0:T], ACT.Gelu).then_inc(gelu_done, 1)

            def gates_out(m, slot, t0, b):
                act.wait_ge(g_done, m + 1)
                nc.scalar.activation(gates[:, ds(slot, QUARTER), ds(t0, BATCH)].rearrange("p e t -> p t e"),
                                     bank[2 + b][:, :].rearrange("p (t w e) -> p t w e", w=2, e=QUARTER)[:, :, 0, :],
                                     ACT.Copy).then_inc(gates_up, 1)

            def coef_hi(c, r, j):
                act.wait_ge(cf_done, c + 1)
                nc.scalar.activation(c_hi[r][:, j, :],
                                     stash[:, ds(c % (AHEAD * GROUP), 1), :].rearrange("p a t -> p (a t)"),
                                     ACT.Copy).then_inc(chi_done, 1)

            for c in range(UP_FIRST):
                stream_hi(U_PRE + 2 * c + HLEAD, 2)
                if c == 3:
                    act.wait_ge(rt_exp_in, 1)
                    nc.scalar.activation(sel[:, 2], sel[:, 2], ACT.Exp).then_inc(rt_exp, 1)
                gelu(c, c % 2, U_PRE + 2 * c + 2, False)
            act.wait_ge(sel_tr, 1)
            nc.scalar.activation(gate_t[:, 0, :], bank[5][:, 0:T], ACT.Copy).then_inc(tabs_copied, 1)
            with act.Fori(0, UP_LOOPS) as i:
                u = U_PRE + 2 * UP_FIRST + 4 * i
                ur = U_PRE + 2 * UP_FIRST
                for b in range(2):
                    for s in range(2):
                        hi(u + 2 * b + HLEAD + s, ur + 2 * b + HLEAD + s)
                    for r in range(2):
                        gates_out(4 * i + 2 * b + r, 0, BATCH * (4 * i + 2 * b + r), r)
                    gelu(UP_FIRST + 2 * i + b, b, u + 2 * b + 2, False)
            for m in range(4 * UP_LOOPS, (GROUPS_Q + 1) * GROUP):
                q = m // (T // BATCH)
                gates_out(m, QUARTER * q, BATCH * m - T * q, m % 2)
            for c in range(GROUP):
                coef_hi(c, 0, c)

            def group(g, par, ups, builds):
                for j in range(GROUP):
                    if ups:
                        u, ur = U_MAIN + GSTEP * g + STEP * j, U_MAIN + STEP * j
                    else:
                        u, ur = U_TAIL + 2 * GROUP * (g - GROUPS + AHEAD) + 2 * j, U_TAIL + 2 * j
                    if not (isinstance(g, int) and g == GROUPS - 1):
                        coef_hi(GROUP * (g + 1) + j, (par + 1) % 2, j)
                    n = STEP if ups else 2
                    for s in range(n):
                        if s == n - 1 and builds:
                            m = GROUP * (g + 1) + j + T // BATCH
                            gates_out(m, QUARTER * (((g + 1) // GROUPS_Q + 1) % 2),
                                      BATCH * (GROUP * ((g + 1) % GROUPS_Q) + j), j % 2)
                        if not (isinstance(u, int) and u + HLEAD + s >= U_END):
                            hi(u + HLEAD + s, ur + HLEAD + s)
                    if ups:
                        gelu(GROUP * (g + AHEAD) + j, j % 2, u + STEP)

            group(0, 0, True, True)
            with act.Fori(0, 11) as p:
                for b in range(2):
                    group(2 * p + 1 + b, 1 + b, True, True)
            for g in range(23, GROUPS - AHEAD):
                group(g, g % 2, True, False)
            with act.Fori((GROUPS - AHEAD) // 2, GROUPS // 2 - 1) as p:
                for b in range(2):
                    group(2 * p + b, b, False, False)
            for g in range(GROUPS - 2, GROUPS):
                group(g, g % 2, False, False)

            for b in range(TB):
                act.wait_ge(ln_var, TB + b + 1)
                nc.scalar.activation(rstd[:, b, :], mv[:, b, 1:2], ACT.Sqrt).then_inc(ln_std, 1)

        @block.vector
        def _(dve):
            tt = nc.vector.tensor_tensor
            ts = nc.vector.tensor_scalar
            stt = nc.vector.scalar_tensor_tensor

            def lo(u, slot_u):
                if slot_u % 2 == 0:
                    dve.wait_ge(hi_done, u + 1)
                    tt(w_lo[slot_u % SPLIT][:, :], raw[:, slot_u % RAW, :], w_hi[slot_u % SPLIT][:, :].bitcast(f32),
                       ALU.subtract).then_inc(lo_even, 2)

            def stream_lo(first, n):
                for u in range(first, first + n):
                    lo(u, u)

            for n, (credit, count) in enumerate(((used, USED0), (glu_done, GLU0), (s_done, S0), (taps_done, TAPS0), (s_ready, SC0),
                                                   (gates_done, GATES0))):
                nc.vector.memset(stats[:, 0, 0, n:n + 1], 0.0).then_inc(credit, count)
            def x_lo(c):
                dve.wait_ge(xhi_done, c + 1)
                tt(xt_lo[:, 4 * c:4 * c + 4, :], xt_raw[:, 4 * c:4 * c + 4, :],
                   xt_hi[:, 4 * c:4 * c + 4, :].bitcast(f32), ALU.subtract).then_inc(xlo_done, 1)

            lo(0, 0)
            for c in range(4):
                x_lo(c)
            lo(2, 2)
            dve.wait_ge(prm_in, 16)
            dve.wait_ge(pool_done, 5)

            def tap(t, k, first_wait):
                a = apad[:, ds(t, 1), k:k + T]
                w = prm[:, ds(PC_CW + TAPS * t + k, 1)]
                s = cacc[:, k % 2, ds(t, 1), :]
                dve.wait_ge(taps_done, TAPS0 + first_wait)
                if k == 0:
                    i = ts(s, a, w, prm[:, ds(PC_CB + t, 1)], ALU.mult, ALU.add)
                elif k == 1:
                    i = ts(s, a, w, None, ALU.mult)
                else:
                    i = stt(s, a, w, s, ALU.mult, ALU.add)
                i.then_inc(taps_done, 1)

            def layer_norm(count, g, b_, done):
                n = [count]

                def link(ins):
                    n[0] += 1
                    ins.then_inc(ln_chain, 1)

                dve.wait_ge(ln_chain, n[0])
                for b in range(TB):
                    link(nc.vector.bn_aggr(mv[:, b, :], stats[:, b, :, :].rearrange("p c s -> p (c s)")))
                dve.wait_ge(ln_chain, n[0])
                for b in range(TB):
                    nc.vector.tensor_scalar_add(mv[:, b, 1:2], mv[:, b, 1:2], EPS).then_inc(ln_var, 1)
                base = TB if done is fin else 0
                chunks = [(d, b) for d in range(NCH) for b in range(TB)]

                def centre(d, b):
                    sl = slice(d * DCH, (d + 1) * DCH)
                    link(stt(acc[:, b, sl], acc[:, b, sl], mv[:, b, 0:1], g[:, sl], ALU.subtract, ALU.mult))
                    return n[0]

                ready = [centre(*chunks[0]), centre(*chunks[1])]
                for b in range(TB):
                    dve.wait_ge(ln_std, base + b + 1)
                    link(nc.vector.reciprocal(rstd[:, b, :], rstd[:, b, :]))
                r = n[0]
                for k, (d, b) in enumerate(chunks):
                    if k + 2 < len(chunks):
                        ready.append(centre(*chunks[k + 2]))
                    sl = slice(d * DCH, (d + 1) * DCH)
                    dve.wait_ge(ln_chain, max(ready[k], r))
                    stt(acc[:, b, sl], acc[:, b, sl], rstd[:, b, :], b_[:, sl], ALU.mult, ALU.add).then_inc(done, 1)
                    if done is x1_done and k >= 2:
                        x1_lo(k - 2)
                if done is x1_done:
                    x1_lo(len(chunks) - 2)
                    x1_lo(len(chunks) - 1)

            def x1_lo(n):
                k4, b = 4 * (n // TB), n % TB
                dve.wait_ge(x1hi_done, n + 1)
                tt(xt_lo[:, k4:k4 + 4, b * P:(b + 1) * P], bank[n][:, :].rearrange("p (k t) -> p k t", t=P),
                   xt_hi[:, k4:k4 + 4, b * P:(b + 1) * P].bitcast(f32), ALU.subtract).then_inc(x1lo_done, 1)

            H1 = 14
            stream_lo(U_CONF + LEAD, 4)
            with dve.Fori(0, CONF_TILES // 2) as i:
                for b in range(2):
                    u = U_CONF + 8 * i + 4 * (b + 1) + LEAD
                    t = 2 * i + b
                    dve.wait_ge(sig_done, t + 1)
                    stt(apad[:, ds(t, 1), TAPS - 1:TAPS - 1 + T].rearrange("p a t -> p (a t)"), bank[b][:, 0:T],
                        prm[:, ds(PC_B + 2 * t, 1)], sig[:, b, :], ALU.add, ALU.mult).then_inc(glu_done, 1)
                    dve.wait_ge(glu_done, GLU0 + t + 1)
                    for s in range(4):
                        for k in range(H1 * s // 4, H1 * (s + 1) // 4):
                            tap(t, k, H1 * t + max(k - 1, 0))
                        lo(u + s, U_CONF + 4 * (b + 1) + LEAD + s)
            dve.wait_ge(xn_in, 16)
            dve.wait_ge(bo_in, 16)
            for b in range(TB):
                stt(acc[:, b, :], acc[:, b, :], ALPHA, bo[:, :], ALU.mult, ALU.add).then_inc(xres_done, 1)
                stream_lo(U_SC + LEAD + 4 + b, 1)
            T1 = H1 * CONF_TILES
            H2 = TAPS - H1
            LO_AT = (1, 4, 7, 10, 13, H2 - 1)
            MIX_AT = 9
            with dve.Fori(0, SC_TILES // 4) as i:
                for b in range(4):
                    u = U_SC + 24 * i + 6 * (b + 1) + LEAD
                    t = 4 * i + b
                    col = PC_B + 2 * CONF_TILES + 3 * t
                    ops = [
                        lambda: stt(scpad[:, 2:2 + T], bank[b % 2][:, 0:T], prm[:, ds(col, 1)], hval[:, b % 2, :],
                                    ALU.add, ALU.mult),
                        lambda: ts(sct[:, 0, :], scpad[:, 0:T], prm[:, ds(PC_SW + 3 * t, 1)],
                                   prm[:, ds(PC_SB + t, 1)], ALU.mult, ALU.add),
                        lambda: stt(sct[:, 1, :], scpad[:, 1:1 + T], prm[:, ds(PC_SW + 3 * t + 1, 1)], sct[:, 0, :],
                                    ALU.mult, ALU.add),
                        lambda: stt(sct[:, 0, :], scpad[:, 2:2 + T], prm[:, ds(PC_SW + 3 * t + 2, 1)], sct[:, 1, :],
                                    ALU.mult, ALU.add),
                        lambda: stt(smix[:, :], bank[4 + b % 2][:, 0:T], prm[:, ds(col + 2, 1)], sct[:, 0, :],
                                    ALU.add, ALU.mult),
                    ]
                    dve.wait_ge(h_done, t + 1)
                    for k in range(H2):
                        if k < len(ops):
                            if k:
                                dve.wait_ge(sc_step, 5 * t + k)
                            ops[k]().then_inc(sc_step, 1)
                        tap(t, H1 + k, T1 + H2 * t + max(k - 1, 0))
                        if k in LO_AT:
                            s = LO_AT.index(k)
                            lo(u + s, U_SC + 6 * (b + 1) + LEAD + s)
                        if k == MIX_AT:
                            dve.wait_ge(s_hi_done, t + 1)
                            tt(mix_lo[:, ds(CONF_TILES + t, 1), :].rearrange("p a t -> p (a t)"), smix[:, :],
                               mix_hi[:, ds(CONF_TILES + t, 1), :].bitcast(f32).rearrange("p a t -> p (a t)"),
                               ALU.subtract).then_inc(s_done, 1)
            o = U_OUT + LEAD
            dve.wait_ge(taps_done, TAPS0 + T1 + H2 * CONF_TILES)
            tt(cacc[:, 0, :, :], cacc[:, 0, :, :], cacc[:, 1, :, :], ALU.add).then_inc(cconv_done, 1)
            stream_lo(o + 6, 3)
            dve.wait_ge(mean_done, 1)
            tt(cacc[:, 0, :, :], cacc[:, 0, :, :], bank[0][:, 0:T].unsqueeze(1).to_broadcast([P, CONF_TILES, T]),
               ALU.subtract).then_inc(cen_done, 1)
            stream_lo(o + 9, 3)
            dve.wait_ge(var_done, 1)
            nc.vector.tensor_scalar_add(lnt[:, 0, :], bank[2][:, 0:T], EPS).then_inc(veps_done, 1)
            stream_lo(o + 12, 1)
            dve.wait_ge(std_done, 1)
            nc.vector.reciprocal(lnt[:, 0, :], lnt[:, 1, :]).then_inc(veps_done, 1)
            dve.wait_ge(veps_done, 2)
            tt(cacc[:, 0, :, :], cacc[:, 0, :, :], lnt[:, 0, :].unsqueeze(1).to_broadcast([P, CONF_TILES, T]),
               ALU.mult).then_inc(cnorm_done, 1)
            stream_lo(o + 13, 1)
            for h in range(2):
                dve.wait_ge(a_hi_done, h + 1)
                tt(mix_lo[:, 4 * h:4 * h + 4, :], cacc[:, 1, 4 * h:4 * h + 4, :],
                   mix_hi[:, 4 * h:4 * h + 4, :].bitcast(f32), ALU.subtract).then_inc(a_lo_done, 1)

            lo_next = o + 14
            dve.wait_ge(xres_done, 2)
            for d in range(NCH):
                end = min(o + 21 + 4 * d, U_Q + LEAD)
                stream_lo(lo_next, end - lo_next)
                lo_next = end
                dve.wait_ge(used, USED0 + U_OUT + 4 * (NCH + d + 1))
                for b in range(TB):
                    sl = acc[:, b, d * DCH:(d + 1) * DCH]
                    tt(sl, y_banks[d][b][:, :], sl, ALU.add).then_inc(ln_chain, 1)
                for b in range(TB):
                    dve.wait_ge(ln_chain, 2 * TB * d + b + 1)
                    nc.vector.bn_stats(stats[:, b, d, :], acc[:, b, d * DCH:(d + 1) * DCH]).then_inc(ln_chain, 1)
            dve.wait_ge(ln1_in, 32)
            layer_norm(2 * TB * NCH, ln_g, ln_b, x1_done)
            dve.wait_ge(x1_tr, 8)
            nc.vector.tensor_scalar_mul(acc[:, :, :], acc[:, :, :], ALPHA).then_inc(xres_done, 1)

            NEG = -3.0e38

            def top16(src, rest, v, idx, first):
                steps = [
                    lambda b: nc.vector.max(v(b, 0), src(b)),
                    lambda b: nc.vector.max_index(idx(b, 0), v(b, 0), src(b)),
                    lambda b: nc.vector.match_replace(rest(b), v(b, 0), src(b), NEG),
                    lambda b: nc.vector.max(v(b, 1), rest(b)),
                    lambda b: nc.vector.max_index(idx(b, 1), v(b, 1), rest(b)),
                ]
                needs = [None, 0, 0, 2, 3]
                for n, step in enumerate(steps):
                    for b in range(TB):
                        if needs[n] is not None:
                            dve.wait_ge(rt, first + 2 * needs[n] + b + 1)
                            dve.nop(nofuse=True)
                        step(b).then_inc(rt, 1)

            dve.wait_ge(iota_done, 1)
            dve.wait_ge(x1lo_done, 8)
            nc.vector.memset(ssum[:, :, :], 0.0).then_inc(rt, PER_HEAD)
            with dve.Fori(0, HEADS // 2) as i:
                for b4 in range(4):
                    u = U_Q + 8 * i + 2 * b4 + LEAD
                    t = 4 * i + b4
                    h = 2 * i + b4 // 2
                    r0 = PER_HEAD * (h + 1) + 11 * (b4 % 2)
                    for s in range(2):
                        lo(u + s, U_Q + 2 * b4 + LEAD + s)
                    dve.wait_ge(s_ready, SC0 + t + 1)
                    dve.nop(nofuse=True)
                    top16(lambda b: bank[2 + b4 % 2][:, b * P:(b + 1) * P],
                          lambda b: srest[:, b, :],
                          lambda b, e: hv[b4 % 2][:, b, 8 * e:8 * e + 8],
                          lambda b, e: hidx[b4 % 2][:, b, 8 * e:8 * e + 8], r0)
                    dve.wait_ge(rt, r0 + 10)
                    nc.vector.tensor_copy(hidx_f[:, :, ds(t, 1), :].rearrange("p b a k -> p b (a k)"),
                                          hidx[b4 % 2][:, :, :]).then_inc(rt, 1)
                    if b4 % 2:
                        r1 = PER_HEAD * (h + 1) + 22
                        dve.wait_ge(rt, r1)
                        for b in range(TB):
                            tt(cand[:, b, :, :],
                               hv[0][:, b, :].unsqueeze(2).to_broadcast([P, TOPK, TOPK]),
                               hv[1][:, b, :].unsqueeze(1).to_broadcast([P, TOPK, TOPK]), ALU.add).then_inc(rt, 1)
                        dve.wait_ge(rt, r1 + 2)
                        dve.nop(nofuse=True)
                        top16(lambda b: cand[:, b, :, :].rearrange("p a k -> p (a k)"),
                              lambda b: crest[:, b, :],
                              lambda b, e: cv[:, b, 8 * e:8 * e + 8],
                              lambda b, e: cidx[:, b, 8 * e:8 * e + 8], r1 + 2)
                        dve.wait_ge(rt, r1 + 12)
                        nc.vector.tensor_copy(tv[:, :, ds(h, 1), :].rearrange("p b a k -> p b (a k)"),
                                              cv[:, :, :]).then_inc(rt, 1)
                        nc.vector.tensor_copy(tci[:, :, ds(h, 1), :].rearrange("p b a k -> p b (a k)"),
                                              cidx[:, :, :]).then_inc(rt, 1)
            R = [PER_HEAD * (HEADS + 1)]

            def link(ins):
                R[0] += 1
                ins.then_inc(rt, 1)

            stream_lo(U_PRE + LEAD, 1)
            dve.wait_ge(rt, R[0])
            tt(sel[:, 2], tv[:, :, :, :], tv[:, :, :, 0:1].to_broadcast([P, TB, HEADS, TOPK]),
               ALU.subtract).then_inc(rt_exp_in, 1)
            link(nc.vector.tensor_single_scalar(tab_u[:, 0], tci[:, :, :, :], 4, ALU.logical_shift_right))
            link(nc.vector.tensor_single_scalar(tab_u[:, 1], tci[:, :, :, :], 15, ALU.bitwise_and))
            dve.wait_ge(rt, R[0])
            link(nc.vector.tensor_copy(tab_f[:, :, :, :, :], tab_u[:, :, :, :, :]))
            stream_lo(U_PRE + LEAD + 1, 1)
            dve.wait_ge(rt, R[0])
            n_eq = 0
            lo_next = U_PRE + LEAD + 2
            for half in range(2):
                for b in range(TB):
                    e = eq[n_eq % 2]
                    n_eq += 1
                    mine = hidx_f[:, b, :, :].rearrange("p (h two) k -> p h two k", two=2)[:, :, half, :]
                    link(tt(e[:, :, :, :], tab_f[:, half, b].unsqueeze(3).to_broadcast([P, HEADS, TOPK, TOPK]),
                            iota[:, 0:TOPK].unsqueeze(1).unsqueeze(1).to_broadcast([P, HEADS, TOPK, TOPK]),
                            ALU.is_equal))
                    stream_lo(lo_next, 1)
                    dve.wait_ge(rt, R[0])
                    link(tt(e[:, :, :, :], e[:, :, :, :], mine.unsqueeze(2).to_broadcast([P, HEADS, TOPK, TOPK]),
                            ALU.mult))
                    stream_lo(lo_next + 1, 1)
                    dve.wait_ge(rt, R[0])
                    link(nc.vector.tensor_reduce(sel[:, half, b], e[:, :, :, :], AX.X, ALU.add))
                    lo_next += 2
            dve.wait_ge(rt_exp, 1)
            link(nc.vector.tensor_reduce(ssum[:, :, :], sel[:, 2], AX.X, ALU.add))
            stream_lo(lo_next, 1)
            dve.wait_ge(rt, R[0])
            link(nc.vector.reciprocal(ssum[:, :, :], ssum[:, :, :]))
            stream_lo(lo_next + 1, 1)
            dve.wait_ge(rt, R[0])
            tt(sel[:, 2], sel[:, 2], ssum[:, :, :].unsqueeze(3).to_broadcast([P, TB, HEADS, TOPK]),
               ALU.mult).then_inc(sel_done, 1)
            lo_next += 2
            stream_lo(lo_next, U_PRE + 2 * UP_FIRST + LEAD - lo_next)
            dve.wait_ge(sel_tr, 1)
            nc.vector.tensor_copy(tab1[:, :], bank[4][:, 0:T]).then_inc(tabs_done, 1)
            nc.vector.tensor_copy(tab2[:, :], bank[4][:, T:2 * T]).then_inc(tabs_done, 1)
            dve.wait_ge(tabs_copied, 1)
            tt(gate_t[:, 1, :], bank[5][:, 0:T], gate_t[:, 0, :].bitcast(f32), ALU.subtract).then_inc(tabs_done, 1)
            dve.wait_ge(tabs_done, 3)

            def onehot2(m, key0, t0):
                if not (isinstance(m, int) and m == 0):
                    dve.wait_ge(oh_chain, m)
                tt(oh2[:, :, :], iota[:, ds(key0, QUARTER)].unsqueeze(1).to_broadcast([P, BATCH, QUARTER]),
                   tab2[:, ds(t0, BATCH)].unsqueeze(2).to_broadcast([P, BATCH, QUARTER]), ALU.is_equal)\
                    .then_inc(oh_first, 1)

            def onehot1(m, t0, b):
                if not (isinstance(m, int) and m < 2):
                    dve.wait_ge(g_done, m - 1)
                tt(oh1[b][:, :, :], iota[:, :].unsqueeze(1).to_broadcast([P, BATCH, P]),
                   tab1[:, ds(t0, BATCH)].unsqueeze(2).to_broadcast([P, BATCH, P]), ALU.is_equal).then_inc(oh_done, 1)

            def gated(m, t0, b):
                dve.wait_ge(oh_first, m + 1)
                tt(oh2g[b][:, :, :, :], oh2[:, :, :].unsqueeze(2).to_broadcast([P, BATCH, 2, QUARTER]),
                   gate_t[:, :, ds(t0, BATCH)].bitcast(f32).rearrange("p w t -> p t w").unsqueeze(3)
                   .to_broadcast([P, BATCH, 2, QUARTER]), ALU.mult).then_inc(oh_chain, 1)

            def build(m, key0, t0, b):
                onehot2(m, key0, t0)
                onehot1(m, t0, b)
                gated(m, t0, b)

            def gates_add(m, slot, t0, b):
                dve.wait_ge(gates_up, m + 1)
                sl = gates[:, ds(slot, QUARTER), ds(t0, BATCH)].rearrange("p e t -> p t e")
                tt(sl, bank[2 + b][:, :].rearrange("p (t w e) -> p t w e", w=2, e=QUARTER)[:, :, 1, :], sl,
                   ALU.add).then_inc(gates_done, 1)

            build(0, 0, 0, 0)
            build(1, 0, BATCH, 1)
            with dve.Fori(0, UP_LOOPS) as i:
                u = U_PRE + 2 * UP_FIRST + 4 * i
                ur = U_PRE + 2 * UP_FIRST
                for b in range(2):
                    m = 4 * i + 2 * b
                    lo(u + LEAD + 2 * b, ur + LEAD + 2 * b)
                    gates_add(m, 0, BATCH * m, 0)
                    build(m + 2, 0, BATCH * m + 2 * BATCH, 0)
                    lo(u + LEAD + 2 * b + 1, ur + LEAD + 2 * b + 1)
                    gates_add(m + 1, 0, BATCH * m + BATCH, 1)
                    build(m + 3, 0, BATCH * m + 3 * BATCH, 1)
            last = (GROUPS_Q + 1) * GROUP
            for m in range(4 * UP_LOOPS, last):
                q, q2 = m // (T // BATCH), (m + 2) // (T // BATCH)
                gates_add(m, QUARTER * q, BATCH * m - T * q, m % 2)
                if m + 2 < last:
                    build(m + 2, QUARTER * q2, BATCH * (m + 2) - T * q2, m % 2)

            def stashed(c):
                return stash[:, ds(c % (AHEAD * GROUP), 1), :].rearrange("p a t -> p (a t)")

            def coef(c, slot, gates_needed):
                dve.wait_ge(gelu_done, c + 1)
                dve.wait_ge(gates_done, GATES0 + gates_needed)
                tt(stashed(c), stashed(c), gates[:, ds(slot, 1), :].rearrange("p a t -> p (a t)"),
                   ALU.mult).then_inc(cf_done, 1)

            def coef_lo(c, r, j):
                dve.wait_ge(chi_done, c + 1)
                tt(c_lo[r][:, j, :], stashed(c), c_hi[r][:, j, :].bitcast(f32), ALU.subtract).then_inc(clo_done, 1)

            dve.wait_ge(xres_done, 3)
            for c in range(GROUP):
                coef(c, c, T // BATCH)
            for c in range(GROUP):
                coef_lo(c, 0, c)

            def add_v(u_next, c, b2):
                dve.wait_ge(used, USED0 + u_next)
                for b in range(TB):
                    sl = acc[:, b, c * DCH:(c + 1) * DCH]
                    i = tt(sl, bank[4 + 2 * (b2 % 2) + b][:, :], sl, ALU.add)
                i.then_inc(acc_done, 1)

            def group(g, par, ups, builds):
                more = not (isinstance(g, int) and g == GROUPS - 1)
                for j in range(GROUP):
                    if ups:
                        u, ur = U_MAIN + GSTEP * g + STEP * j, U_MAIN + STEP * j
                    else:
                        u, ur = U_TAIL + 2 * GROUP * (g - GROUPS + AHEAD) + 2 * j, U_TAIL + 2 * j
                    m = GROUP * (g + 1) + j + T // BATCH
                    t0 = BATCH * (GROUP * ((g + 1) % GROUPS_Q) + j)
                    slot = QUARTER * (((g + 1) // GROUPS_Q + 1) % 2)
                    c = GROUP * (g + 1) + j

                    def split(s):
                        if not (isinstance(u, int) and u + LEAD + s >= U_END):
                            lo(u + LEAD + s, ur + LEAD + s)

                    if more:
                        coef(c, GROUP * ((g + 1) % (2 * GROUPS_Q)) + j, (T // BATCH) * ((g + 1) // GROUPS_Q + 1))
                    if builds:
                        onehot2(m, QUARTER * ((g + 1) // GROUPS_Q + 1), t0)
                    split(0)
                    if more:
                        coef_lo(c, (par + 1) % 2, j)
                    if builds:
                        onehot1(m, t0, j % 2)
                    split(1)
                    if builds:
                        gated(m, t0, j % 2)
                    if ups:
                        split(2)
                    add_v(u + 2, j, j)
                    if ups:
                        split(3)
                    if builds:
                        gates_add(m, slot, t0, j % 2)

            group(0, 0, True, True)
            with dve.Fori(0, 11) as p:
                for b in range(2):
                    group(2 * p + 1 + b, 1 + b, True, True)
            for g in range(23, GROUPS - AHEAD):
                group(g, g % 2, True, False)
            with dve.Fori((GROUPS - AHEAD) // 2, GROUPS // 2 - 1) as p:
                for b in range(2):
                    group(2 * p + b, b, False, False)
            for g in range(GROUPS - 2, GROUPS):
                group(g, g % 2, False, False)
            dve.wait_ge(acc_done, GROUPS * GROUP)
            for b in range(TB):
                for d in range(NCH):
                    nc.vector.bn_stats(stats[:, b, d, :], acc[:, b, d * DCH:(d + 1) * DCH]).then_inc(ln_chain, 1)
            dve.wait_ge(ln2_in, 32)
            layer_norm(2 * TB * NCH + 2 * TB + TB * NCH + TB * NCH, ln2g, ln2b, fin)

        @block.tensor
        def _(pe):
            mm = nc.tensor.matmul

            def stationary_unit(u, slot_u, half, dst):
                wait_lo(pe, u, slot_u)
                hi_w, lo_w = w_hi[slot_u % SPLIT], w_lo[slot_u % SPLIT]
                for k in range(HALF):
                    kk = HALF * half + k
                    sl = slice(k * P, (k + 1) * P)
                    st, en = half == 0 and k == 0, half == 1 and k == HALF - 1
                    mm(dst, hi_w[:, sl], xt_hi[:, kk, :], start=st, stop=False)
                    mm(dst, hi_w[:, sl], xt_lo[:, kk, :], start=False, stop=False)
                    i = mm(dst, lo_w[:, sl], xt_hi[:, kk, :], start=False, stop=en)
                i.then_inc(used, 1)

            with pe.Fori(0, CONF_TILES // 2) as i:
                for b in range(2):
                    t = 2 * i + b
                    pe.wait_ge(glu_done, GLU0 + t - 1)
                    for w in range(2):
                        for h in range(2):
                            n = 4 * b + 2 * w + h
                            pe.wait_ge(xlo_done, 2 * h + 2)
                            stationary_unit(U_CONF + 8 * i + n, U_CONF + n, h, bank[2 * w + b][:, 0:T])
            with pe.Fori(0, SC_TILES // 4) as i:
                for b in range(4):
                    t = 4 * i + b
                    if b < 2:
                        pe.wait_ge(glu_done, GLU0 + CONF_TILES)
                    pe.wait_ge(s_done, S0 + t - 1)
                    for w in range(3):
                        for h in range(2):
                            n = 6 * b + 2 * w + h
                            stationary_unit(U_SC + 24 * i + n, U_SC + n, h, bank[2 * w + b % 2][:, 0:T])

            def out_units(u0, k0, d, first, last):
                for n in range(4):
                    wait_lo(pe, u0 + n, u0 + n)
                    hi_w, lo_w = w_hi[(u0 + n) % SPLIT], w_lo[(u0 + n) % SPLIT]
                    for k in range(2):
                        kk = k0 + 2 * n + k
                        if u0 < U_OUT + 4:
                            pe.wait_ge(s_done, S0 + kk - CONF_TILES + 1)
                        st, en = first and n == 0 and k == 0, last and n == 3 and k == 1
                        w1, w2 = hi_w[:, k * DCH:(k + 1) * DCH], lo_w[:, k * DCH:(k + 1) * DCH]
                        for b in range(TB):
                            a1, a2 = mix_hi[:, kk, b * P:(b + 1) * P], mix_lo[:, kk, b * P:(b + 1) * P]
                            dst = y_banks[d][b][:, :]
                            mm(dst, a1, w1, start=st, stop=False)
                            mm(dst, a1, w2, start=False, stop=False)
                            i = mm(dst, a2, w1, start=False, stop=en)
                    i.then_inc(used, 1)

            for d in range(2):
                out_units(U_OUT + 4 * d, CONF_TILES, d, True, False)
            pe.wait_ge(cconv_done, 1)
            for t in range(CONF_TILES):
                i = mm(bank[0][:, 0:T], ones[:, :], cacc[:, 0, t, :], start=t == 0, stop=t == CONF_TILES - 1)
            i.then_inc(mean_done, 1)
            out_units(U_OUT + 8, CONF_TILES, 2, True, False)
            pe.wait_ge(sq_done, 1)
            for t in range(CONF_TILES):
                i = mm(bank[2][:, 0:T], ones[:, :], cacc[:, 1, t, :], start=t == 0, stop=t == CONF_TILES - 1)
            i.then_inc(var_done, 1)
            pe.wait_ge(veps_done, 1)
            out_units(U_OUT + 12, CONF_TILES, 3, True, False)
            pe.wait_ge(a_lo_done, 2)
            for d in range(NCH):
                out_units(U_OUT + 16 + 4 * d, 0, d, False, True)
            pe.wait_ge(pool_done, 5)
            for n in range(8):
                k4, b = 4 * (n // TB), n % TB
                pe.wait_ge(x1_done, n + 1)
                for k in range(4):
                    i = nc.tensor.transpose(bank[n][:, k * P:(k + 1) * P], acc[:, b, (k4 + k) * P:(k4 + k + 1) * P],
                                            ident[:, :])
                i.then_inc(x1_tr, 1)
            pe.wait_ge(keys_in, 16)

            def scores(t, b4, h_pair):
                pe.wait_ge(qt_done, t + 1)
                pe.wait_ge(rt, PER_HEAD * (2 * h_pair + b4 // 2) + 11 * (b4 % 2) + 6)
                for b in range(TB):
                    i = mm(bank[2 + b4 % 2][:, b * P:(b + 1) * P], q_t[b4 % 2][:, b * P:(b + 1) * P],
                           keys[:, ds(N_KEYS * t, N_KEYS)], start=True, stop=True)
                i.then_inc(s_ready, 1)

            with pe.Fori(0, HEADS // 2) as i:
                for b4 in range(4):
                    t = 4 * i + b4
                    n = 2 * b4
                    if b4 == 0:
                        pe.wait_ge(x1lo_done, 4)
                    stationary_unit(U_Q + 8 * i + n, U_Q + n, 0, bank[b4 % 2][:, 0:T])
                    if b4 == 0:
                        pe.wait_ge(x1lo_done, 8)
                    if b4:
                        scores(t - 1, b4 - 1, i)
                    stationary_unit(U_Q + 8 * i + n + 1, U_Q + n + 1, 1, bank[b4 % 2][:, 0:T])
                scores(4 * i + 3, 3, i)

            def up(c, c_ring, u, ur, between=None):
                if not (isinstance(c, int) and c < 2):
                    pe.wait_ge(gelu_done, c - 1)
                for h in range(2):
                    stationary_unit(u + h, ur + h, h, bank[c_ring % 2][:, 0:T])
                    if h == 0 and between:
                        between()

            for c in range(UP_FIRST):
                up(c, c, U_PRE + 2 * c, U_PRE + 2 * c)

            pe.wait_ge(sel_done, 1)
            for w in range(3):
                dst = bank[4 + w // 2]
                for b in range(TB):
                    i = nc.tensor.transpose(dst[:, (w % 2) * T + b * P:(w % 2) * T + (b + 1) * P],
                                            sel[:, w, b].rearrange("p h k -> p (h k)"), ident[:, :])
            i.then_inc(sel_tr, 1)

            def gate_batch(m, b):
                pe.wait_ge(oh_done, m + 1)
                pe.wait_ge(oh_chain, m + 1)
                if not (isinstance(m, int) and m < 2):
                    pe.wait_ge(gates_done, GATES0 + m - 1)
                for t in range(BATCH):
                    i = mm(bank[2 + b][:, 2 * t * QUARTER:2 * (t + 1) * QUARTER], oh1[b][:, t, :],
                           oh2g[b][:, t, :, :].rearrange("p w e -> p (w e)"), start=True, stop=True)
                i.then_inc(g_done, 1)

            with pe.Fori(0, UP_LOOPS) as i:
                for b in range(2):
                    c = UP_FIRST + 2 * i + b
                    up(c, b, U_PRE + 2 * UP_FIRST + 4 * i + 2 * b, U_PRE + 2 * UP_FIRST + 2 * b)
                    for r in range(2):
                        gate_batch(4 * i + 2 * b + r, r)
            for m in range(4 * UP_LOOPS, (GROUPS_Q + 1) * GROUP):
                gate_batch(m, m % 2)

            def down(n, par, j, u, ur, free):
                if free:
                    pe.wait_ge(acc_done, n - 1)
                for h in range(2):
                    wait_lo(pe, u + h, ur + h)
                    hi_w, lo_w = w_hi[(ur + h) % SPLIT], w_lo[(ur + h) % SPLIT]
                    for e in range(2):
                        w1, w2 = hi_w[:, e * DCH:(e + 1) * DCH], lo_w[:, e * DCH:(e + 1) * DCH]
                        for b in range(TB):
                            dst = bank[4 + 2 * (j % 2) + b][:, :]
                            a1 = c_hi[par][:, 2 * h + e, b * P:(b + 1) * P]
                            a2 = c_lo[par][:, 2 * h + e, b * P:(b + 1) * P]
                            mm(dst, a1, w1, start=h == 0 and e == 0, stop=False)
                            mm(dst, a1, w2, start=False, stop=False)
                            i = mm(dst, a2, w1, start=False, stop=h == 1 and e == 1)
                    i.then_inc(used, 1)

            def group(g, par, ups, builds):
                first = isinstance(g, int) and g == 0
                for j in range(GROUP):
                    if ups:
                        u, ur = U_MAIN + GSTEP * g + STEP * j, U_MAIN + STEP * j
                    else:
                        u, ur = U_TAIL + 2 * GROUP * (g - GROUPS + AHEAD) + 2 * j, U_TAIL + 2 * j
                    if j == 0:
                        pe.wait_ge(clo_done, GROUP * (g + 1))
                    down(GROUP * g + j, par % 2, j, u, ur, not (first and j < 2))
                    if ups:
                        up(GROUP * (g + AHEAD) + j, j, u + 2, ur + 2,
                           (lambda: gate_batch(GROUP * (g + 1) + j + T // BATCH, j % 2)) if builds else None)

            group(0, 0, True, True)
            with pe.Fori(0, 11) as p:
                for b in range(2):
                    group(2 * p + 1 + b, 1 + b, True, True)
            for g in range(23, GROUPS - AHEAD):
                group(g, g % 2, True, False)
            with pe.Fori((GROUPS - AHEAD) // 2, GROUPS // 2 - 1) as p:
                for b in range(2):
                    group(2 * p + b, b, False, False)
            for g in range(GROUPS - 2, GROUPS):
                group(g, g % 2, False, False)


_OUT_SHAPE = (1, T, D)


def kernel(**inputs):
    import numpy as _np
    import concourse.bacc as _bacc
    from concourse import mybir as _mybir
    from concourse.bass_utils import run_bass_kernel_spmd as _run

    a = {name: _np.asarray(value) for name, value in inputs.items()}
    c, s = CONF_TILES, SC_TILES
    order = [t for i in range(c) for t in (i, c + i)] + [2 * c + t for i in range(s) for t in (s + i, 2 * s + i, i)]

    def stationary_units(w):
        n = w.shape[1] // P
        return w.reshape(2, HALF, P, n, P).transpose(3, 0, 2, 1, 4)

    w_in = stationary_units(a["w_in"][0])[order]
    w_q = stationary_units(a["w_q"][0])
    u_w = a["peer_u"][0].reshape(N_KEYS, N_KEYS, 2, HALF, P).transpose(1, 2, 4, 3, 0)
    v_w = a["peer_v"][0].reshape(N_KEYS, GROUPS, 2, 2, NCH, DCH).transpose(1, 4, 2, 0, 3, 5)
    w_out = a["w_out"][0].reshape(2, 4, 2, P, NCH, DCH).transpose(4, 0, 1, 3, 2, 5)
    w_out = w_out.transpose(1, 0, 2, 3, 4, 5)[::-1]
    cols = [a["b_in"][0].reshape(-1, P)[order].T,
            a["conf_conv_w"][0].reshape(TAPS, c, P).transpose(2, 1, 0).reshape(P, -1),
            a["conf_conv_b"][0].reshape(c, P).T, a["conf_ln_g"][0].reshape(c, P).T, a["conf_ln_b"][0].reshape(c, P).T,
            a["sc_conv_w"][0].reshape(SC_TAPS, s, P).transpose(2, 1, 0).reshape(P, -1),
            a["sc_conv_b"][0].reshape(s, P).T]
    laid = {
        "x_t": a["x"][0].reshape(T, KT, P).transpose(2, 1, 0),
        "x_nat": a["x"][0],
        "w_in": w_in.reshape(-1, P, HALF * P),
        "w_out": w_out.reshape(-1, P, HALF * P),
        "w_q": w_q.reshape(-1, P, HALF * P),
        "u_w": u_w.reshape(-1, P, HALF * P),
        "v_w": v_w.reshape(-1, P, HALF * P),
        "params": _np.concatenate(cols, axis=1),
        "sub_keys": a["sub_keys"][0].transpose(3, 0, 1, 2).reshape(P, -1),
    }
    for name in ("b_out", "ln1_g", "ln1_b", "ln2_g", "ln2_b"):
        laid[name] = a[name].reshape(1, D)

    nc = _bacc.Bacc("TRN2", target_bir_lowering=False, num_devices=1, dynamic_dma_scratch_size=1024)
    arrays, args = {}, []
    for name, value in laid.items():
        value = _np.ascontiguousarray(value)
        arrays[f"in_{name}_dram"] = value
        args.append(nc.dram_tensor(f"in_{name}_dram", value.shape, _mybir.dt.from_np(value.dtype),
                                   kind="ExternalInput").ap())
    args.append(nc.dram_tensor("out_dram", _OUT_SHAPE[1:], _mybir.dt.float32, kind="ExternalOutput").ap())
    build(nc, *args)
    r = _run(nc, [arrays], core_ids=[0])
    return r.results[0]["out_dram"].reshape(_OUT_SHAPE)
```

```python
import concourse.bass as bass
from concourse import mybir
from contextlib import ExitStack

P = 128
T = 256
TB = T // P
D = 2048
KT = D // P
HALF = KT // 2
CONF_TILES = 8
SC_TILES = 8
TAPS = 31
SC_TAPS = 3
HEADS = 8
TOPK = 16
N_KEYS = 128
DCH = 512
NCH = D // DCH
GROUP = 4
GROUPS = N_KEYS // GROUP
QUARTER = 32
GROUPS_Q = QUARTER // GROUP
BATCH = 8
PARTS = 2
LOWER = 2.0 ** 11
EXPONENT = 0x7F800000
FRACTION = 0x007FFFFF
ONE = 0x3F800000
ALPHA = 2.0 ** 0.25
EPS = 1e-5
RAW = 4
SPLIT = 4
LEAD = 3
HLEAD = LEAD + 1
AHEAD = 6
UP_FIRST = 8
UP_LOOPS = 8

U_CONF = 0
U_SC = U_CONF + 2 * 2 * CONF_TILES
U_OUT = U_SC + 3 * 2 * SC_TILES
U_Q = U_OUT + NCH * HALF
U_PRE = U_Q + 2 * 2 * HEADS
U_MAIN = U_PRE + AHEAD * GROUP * 2
STEP = 4
GSTEP = GROUP * STEP
U_TAIL = U_MAIN + (GROUPS - AHEAD) * GSTEP
U_END = U_TAIL + AHEAD * 2 * GROUP
X1_ORDER = [(0, 0), (0, 1), (0, 2), (1, 0), (1, 1), (0, 3), (1, 2), (1, 3)]
X1_HALF = 5
LN2_VECTOR = [(0, 0), (0, 1), (1, 0), (1, 1), (1, 2)]
LN2_POOL = [(0, 3), (0, 2), (1, 3)]
PC_B = 0
PC_CW = PC_B + 2 * CONF_TILES + 3 * SC_TILES
PC_CB = PC_CW + CONF_TILES * TAPS
PC_LG = PC_CB + CONF_TILES
PC_LB = PC_LG + CONF_TILES
PC_SW = PC_LB + CONF_TILES
PC_SB = PC_SW + SC_TILES * SC_TAPS
PC_END = PC_SB + SC_TILES


def build(nc, x_t, x_nat, w_in, w_out, w_q, u_w, v_w, params, sub_keys, b_out, ln1_g, ln1_b, ln2_g, ln2_b, out):
    f32 = mybir.dt.float32
    f32r = mybir.dt.float32r
    bf16 = mybir.dt.bfloat16
    f16 = mybir.dt.float16
    u32 = mybir.dt.uint32
    ALU = mybir.AluOpType
    ACT = mybir.ActivationFunctionType
    AX = mybir.AxisListType
    ds = bass.ds

    ctx = ExitStack()
    with ctx:
        def sb(name, shape, dt, where=ctx):
            return where.enter_context(nc.sbuf_tensor(name, shape, dt))

        def sem(name):
            return ctx.enter_context(nc.semaphore(name))

        raw = sb("raw", [P, RAW, HALF * P], f32)
        w_hi = [sb(f"w_hi{i}", [P, HALF * P], f32r) for i in range(SPLIT)]
        w_lo = [sb(f"w_lo{i}", [P, HALF * P], f32r) for i in range(SPLIT)]
        xt_hi = sb("xt_hi", [P, KT, T], f32r)
        xt_lo = sb("xt_lo", [P, KT, T], f32r)
        acc = sb("acc", [P, TB, D], f32)
        iota = sb("iota", [P, P], f32)
        iota_t = sb("iota_t", [P, P, BATCH], f16)
        ident = sb("ident", [P, P], f32)
        stats = sb("stats", [P, TB, NCH, 6], f32)
        mv = sb("mv", [P, TB, 2], f32)
        rstd = sb("rstd", [P, TB, 1], f32)
        neg_mean = sb("neg_mean", [P, TB, 1], f32)
        early = ExitStack()
        keys = sb("keys", [P, 2 * HEADS * N_KEYS], f32, early)
        xt_raw = sb("xt_raw", [P, KT, T], f32, early)
        prm = sb("prm", [P, PC_END], f32, early)
        apad = sb("apad", [P, CONF_TILES, TAPS - 1 + T], f32, early)
        cacc = sb("cacc", [P, 2, CONF_TILES, T], f32, early)
        mix_hi = sb("mix_hi", [P, KT, T], f32r, early)
        mix_lo = sb("mix_lo", [P, KT, T], f32r, early)
        scpad = sb("scpad", [P, SC_TAPS - 1 + T], f32, early)
        sct = sb("sct", [P, 2, T], f32, early)
        sig = sb("sig", [P, 2, T], f32, early)
        hval = sb("hval", [P, 2, T], f32, early)
        smix = sb("smix", [P, T], f32, early)
        ones = sb("ones", [P, P], f32, early)
        lnt = sb("lnt", [P, 2, T], f32, early)
        ln_g = xt_raw[:, 0:8, :].rearrange("p a b -> p (a b)")
        ln_b = xt_raw[:, 8:16, :].rearrange("p a b -> p (a b)")
        bo = sb("bo", [P, D], f32, early)
        early.close()
        c_hi = [sb(f"c_hi{i}", [P, GROUP, T], f32r) for i in range(2)]
        c_lo = [sb(f"c_lo{i}", [P, GROUP, T], f32r) for i in range(2)]
        tab1 = sb("tab1", [P, T], f16)
        tab2 = sb("tab2", [P, T], f16)
        gate = sb("gate", [P, T], f32)
        gate_e = sb("gate_e", [P, T], u32)
        gate_p = sb("gate_p", [P, T], bf16)
        gate_m = sb("gate_m", [P, T], u32)
        gate_t = sb("gate_t", [P, PARTS, T], f16)
        gate_r = sb("gate_r", [P, T], f32)
        stash = sb("stash", [P, AHEAD * GROUP, T], f32)
        oh1 = [sb(f"oh1_{i}", [P, P, BATCH], bf16) for i in range(2)]
        oh2 = sb("oh2", [P, QUARTER, BATCH], f16)
        oh2g = [sb(f"oh2g_{i}", [P, PARTS, QUARTER, BATCH], f16) for i in range(2)]
        route = ExitStack()
        q_t = [sb(f"q_t{i}", [P, T], f32, route) for i in range(2)]
        srest = sb("srest", [P, TB, N_KEYS], f32, route)
        cand = sb("cand", [P, TB, TOPK, TOPK], f32, route)
        crest = sb("crest", [P, TB, TOPK * TOPK], f32, route)
        hv = [sb(f"hv{i}", [P, TB, TOPK], f32, route) for i in range(2)]
        hidx = [sb(f"hidx{i}", [P, TB, TOPK], u32, route) for i in range(2)]
        cv = sb("cv", [P, TB, TOPK], f32, route)
        cidx = sb("cidx", [P, TB, TOPK], u32, route)
        hidx_f = sb("hidx_f", [P, TB, 2 * HEADS, TOPK], bf16, route)
        tv = sb("tv", [P, TB, HEADS, TOPK], f32, route)
        tci = sb("tci", [P, TB, HEADS, TOPK], u32, route)
        tab_u = sb("tab_u", [P, 2, TB, HEADS, TOPK], u32, route)
        tab_f = sb("tab_f", [P, 2, TB, HEADS, TOPK], bf16, route)
        iota16 = sb("iota16", [P, TOPK, TOPK], bf16, route)
        eq = [sb(f"eq{i}", [P, HEADS, TOPK, TOPK], bf16, route) for i in range(2)]
        sel = sb("sel", [P, 3, TB, HEADS, TOPK], f32, route)
        ssum = sb("ssum", [P, TB, HEADS], f32, route)
        route.close()
        gates = sb("gates", [P, 2 * QUARTER, T], f32)
        ln2g = gates[:, 0:8, :].rearrange("p a b -> p (a b)")
        ln2b = gates[:, 8:16, :].rearrange("p a b -> p (a b)")

        bank = [ctx.enter_context(nc.psum_tensor(f"bank{i}", [P, DCH], f32)) for i in range(8)]

        y_banks = [[bank[6], bank[7]], [bank[4], bank[5]], [bank[1], bank[3]], [bank[0], bank[2]]]

        def x1_bank(b, d):
            return bank[d if b else NCH + d]

        USED0, GLU0, S0, TAPS0, SC0, GATES0 = 1, 2, 2, 1, 1, 2

        raw_in = [sem(f"raw_in{i}") for i in range(RAW)]
        hi_done = sem("hi_done")
        lo_done = [sem(f"lo_done{i}") for i in range(SPLIT)]
        used = sem("used")
        xt_in = [sem(f"xt_in{i}") for i in range(4)]
        prm_in = sem("prm_in")
        xn_in = sem("xn_in")
        bo_in = sem("bo_in")
        xhi_done = sem("xhi_done")
        xlo_done = sem("xlo_done")
        pool_done = sem("pool_done")
        iota_done = sem("iota_done")
        sig_done = sem("sig_done")
        glu_done = sem("glu_done")
        taps_done = sem("taps_done")
        h_done = sem("h_done")
        sc_step = sem("sc_step")
        s_hi_done = sem("s_hi_done")
        s_done = sem("s_done")
        cconv_done = sem("cconv_done")
        csum_done = sem("csum_done")
        sqsum_done = sem("sqsum_done")
        mean_done = sem("mean_done")
        sq_done = sem("sq_done")
        cen_done = sem("cen_done")
        var_done = sem("var_done")
        veps_done = sem("veps_done")
        std_done = sem("std_done")
        cnorm_done = sem("cnorm_done")
        silu_done = sem("silu_done")
        a_hi_done = sem("a_hi_done")
        a_lo_done = sem("a_lo_done")
        xres_done = sem("xres_done")
        ln_chain = sem("ln_chain")
        ln_var = sem("ln_var")
        ln_std = sem("ln_std")
        ln1_in = sem("ln1_in")
        x1_done = sem("x1_done")
        x1_tr = sem("x1_tr")
        x1hi_done = sem("x1hi_done")
        x1lo_done = sem("x1lo_done")
        keys_in = sem("keys_in")
        qt_done = sem("qt_done")
        s_ready = sem("s_ready")
        rt = sem("rt")
        rt_exp_in = sem("rt_exp_in")
        rt_exp = sem("rt_exp")
        sel_done = sem("sel_done")
        sel_tr = sem("sel_tr")
        tabs_copied = sem("tabs_copied")
        tabs_done = sem("tabs_done")
        gelu_done = sem("gelu_done")
        oh_first = sem("oh_first")
        oh_chain = sem("oh_chain")
        oh1_first = sem("oh1_first")
        oh_done = sem("oh_done")
        g_done = sem("g_done")
        gates_up = sem("gates_up")
        gates_done = sem("gates_done")
        cf_done = sem("cf_done")
        chi_done = sem("chi_done")
        clo_done = sem("clo_done")
        acc_done = sem("acc_done")
        ln2_in = sem("ln2_in")
        ln2_rstd = sem("ln2_rstd")
        neg_done = sem("neg_done")
        normed = sem("normed")
        pool_ln = sem("pool_ln")
        fin = sem("fin")
        fin_pool = sem("fin_pool")
        y0_done = sem("y0_done")
        v0_done = sem("v0_done")
        out_done = sem("out_done")

        block = ctx.enter_context(nc.Block())

        PER_HEAD = 2 * 11 + 2 + 12

        def batches(g, j):
            if isinstance(g, int) and g == 0:
                for r in range(2):
                    n = 2 * j + r
                    yield n + T // BATCH, QUARTER, QUARTER, BATCH * n, n % 2
            else:
                q = (g + 1) // GROUPS_Q + 1
                n = GROUP * ((g + 1) % GROUPS_Q) + j
                yield GROUP * (g + 1) + j + T // BATCH, QUARTER * q, QUARTER * (q % 2), BATCH * n, j % 2

        def wait_lo(engine, u, slot_u):
            slot = slot_u % SPLIT
            engine.wait_ge(lo_done[slot], u - slot + SPLIT)

        def vector_takes(u):
            if U_Q <= u < U_PRE + 2 * UP_FIRST:
                return u % SPLIT == 0 and u != U_Q
            return u % 2 == 0

        @block.sync
        def _(sp):
            def load(slot, src, u=None):
                if u is not None:
                    wait_lo(sp, u - RAW, slot)
                sp.dma_start(raw[:, slot, :], src).then_inc(raw_in[slot], 16)

            def load_x(c):
                sp.dma_start(xt_raw[:, 4 * c:4 * c + 4, :], x_t[:, 4 * c:4 * c + 4, :]).then_inc(xt_in[c], 16)

            load(0, w_in[0])
            load_x(0)
            load_x(1)
            load(1, w_in[1])
            load_x(2)
            load_x(3)
            load(2, w_in[2])
            load(3, w_in[3])

            def stream(src, base, first, end):
                with sp.Fori(first // RAW, end // RAW) as i:
                    for s in range(RAW):
                        load(s, src[RAW * i + s], base + RAW * i + s)

            stream(w_in, 0, RAW, 4 * RAW)
            sp.dma_start(acc[:, :, :], x_nat.rearrange("(b p) d -> p b d", p=P)).then_inc(xn_in, 16)
            stream(w_in, 0, 4 * RAW, 7 * RAW)
            sp.dma_start(bo[:, :], b_out.to_broadcast([P, D])).then_inc(bo_in, 16)
            stream(w_in, 0, 7 * RAW, 10 * RAW)
            sp.dma_start(keys[:, :], sub_keys).then_inc(keys_in, 16)
            stream(w_in, 0, 10 * RAW, U_OUT)
            stream(w_out, U_OUT, 0, U_Q - U_OUT)
            for dst, src in ((ln_g, ln1_g), (ln_b, ln1_b)):
                sp.dma_start(dst, src.to_broadcast([P, D])).then_inc(ln1_in, 16)
            stream(w_q, U_Q, 0, U_PRE - U_Q)
            stream(u_w, U_PRE, 0, U_MAIN - U_PRE)
            with sp.Fori(0, (U_TAIL - U_MAIN) // STEP) as i:
                for s in range(STEP):
                    load(s, v_w[2 * i + s] if s < 2 else u_w[2 * AHEAD * GROUP + 2 * i + s - 2],
                         U_MAIN + STEP * i + s)
            with sp.Fori(0, (U_END - U_TAIL) // RAW) as i:
                for s in range(RAW):
                    load(s, v_w[2 * GROUP * (GROUPS - AHEAD) + RAW * i + s], U_TAIL + RAW * i + s)
            sp.wait_ge(cf_done, 24 * GROUP)
            for dst, src in ((ln2g, ln2_g), (ln2b, ln2_b)):
                sp.dma_start(dst, src.to_broadcast([P, D])).then_inc(ln2_in, 16)
            for n, (b, d) in enumerate(LN2_VECTOR):
                sp.wait_ge(fin, n + 1)
                sp.dma_start(out[b * P:(b + 1) * P, d * DCH:(d + 1) * DCH],
                             acc[:, b, d * DCH:(d + 1) * DCH]).then_inc(out_done, 16)
            sp.wait_ge(out_done, 16 * NCH * TB)

        @block.gpsimd
        def _(pool):
            nc.gpsimd.iota(iota[:, :], [[1, P]], base=0, channel_multiplier=0,
                           allow_small_or_imprecise_dtypes=True).then_inc(iota_done, 1)
            pool.wait_ge(iota_done, 1)
            nc.gpsimd.tensor_copy(iota_t[:, :, :], iota[:, :].unsqueeze(2).to_broadcast([P, P, BATCH]))\
                .then_inc(iota_done, 1)
            nc.gpsimd.memset(ident[:, :], 0.0).then_inc(pool_done, 1)
            nc.gpsimd.memset(ones[:, :], 1.0 / (CONF_TILES * P)).then_inc(pool_done, 1)
            nc.gpsimd.memset(apad[:, :, 0:TAPS - 1], 0.0).then_inc(pool_done, 1)
            nc.gpsimd.memset(scpad[:, 0:SC_TAPS - 1], 0.0).then_inc(pool_done, 1)
            pool.wait_ge(pool_done, 4)
            nc.gpsimd.affine_select(out=ident[:, :], in_=ident[:, :], compare_op=ALU.not_equal, fill=1.0,
                                    base=0, pattern=[[-1, P]], channel_multiplier=1).then_inc(pool_done, 1)

            def stream_rest(first, end):
                assert first % RAW == 0 and end % RAW == 0
                with pool.Fori(first // RAW, end // RAW) as i:
                    for s in range(RAW):
                        if not vector_takes(end - RAW + s):
                            pool.wait_ge(hi_done, RAW * i + s + 1)
                            nc.gpsimd.tensor_tensor(w_lo[s][:, :], raw[:, s, :], w_hi[s][:, :].bitcast(f32),
                                                    ALU.subtract).then_inc(lo_done[s], SPLIT)

            stream_rest(0, U_Q)
            pool.wait_ge(hi_done, U_Q + 1)
            nc.gpsimd.tensor_tensor(w_lo[0][:, :], raw[:, 0, :], w_hi[0][:, :].bitcast(f32),
                                    ALU.subtract).then_inc(lo_done[0], SPLIT)
            stream_rest(U_Q, U_PRE + 2 * UP_FIRST)
            stream_rest(U_PRE + 2 * UP_FIRST, U_END)
            pool.wait_ge(ln2_in, 32)
            for n, (b, d) in enumerate(LN2_POOL):
                sl = slice(d * DCH, (d + 1) * DCH)
                pool.wait_ge(normed, 2 * n + 2)
                nc.gpsimd.tensor_tensor(acc[:, b, sl], acc[:, b, sl], ln2g[:, sl], ALU.mult).then_inc(pool_ln, 1)
                pool.wait_ge(pool_ln, n + 1)
                nc.gpsimd.tensor_tensor(acc[:, b, sl], acc[:, b, sl], ln2b[:, sl], ALU.add).then_inc(fin_pool, 1)

        @block.scalar
        def _(act):
            def hi(u, slot_u):
                act.wait_ge(raw_in[slot_u % RAW], 16 // RAW * (u - slot_u % RAW) + 16)
                if not isinstance(u, int) or u >= SPLIT:
                    act.wait_ge(used, USED0 + u - (SPLIT - 1))
                nc.scalar.activation(w_hi[slot_u % SPLIT][:, :], raw[:, slot_u % RAW, :], ACT.Copy).then_inc(hi_done, 1)

            def x_hi(c):
                act.wait_ge(xt_in[c], 16)
                nc.scalar.activation(xt_hi[:, 4 * c:4 * c + 4, :], xt_raw[:, 4 * c:4 * c + 4, :],
                                     ACT.Copy).then_inc(xhi_done, 1)

            hi(0, 0)
            act.dma_start(prm[:, :], params).then_inc(prm_in, 16)
            x_hi(0)
            x_hi(1)
            hi(1, 1)
            x_hi(2)
            x_hi(3)
            hi(2, 2)
            hi(3, 3)
            act.wait_ge(prm_in, 16)
            with act.Fori(0, CONF_TILES // 2) as i:
                for b in range(2):
                    u = U_CONF + 8 * i + 4 * b
                    t = 2 * i + b
                    for s in range(3):
                        hi(u + HLEAD + s, U_CONF + 4 * b + HLEAD + s)
                    act.wait_ge(used, USED0 + u + 4)
                    act.wait_ge(glu_done, GLU0 + t - 1)
                    nc.scalar.activation(sig[:, b, :], bank[2 + b][:, 0:T], ACT.Sigmoid,
                                         bias=prm[:, ds(PC_B + 2 * t + 1, 1)]).then_inc(sig_done, 1)
                    hi(u + HLEAD + 3, U_CONF + 4 * b + HLEAD + 3)
            for s in range(2):
                hi(U_SC + HLEAD + s, U_SC + HLEAD + s)
            with act.Fori(0, SC_TILES // 4) as i:
                for b in range(4):
                    u = U_SC + 24 * i + 6 * b
                    t = 4 * i + b
                    for s in range(2, 5):
                        hi(u + HLEAD + s, U_SC + 6 * b + HLEAD + s)
                    act.wait_ge(used, USED0 + u + 6)
                    act.wait_ge(s_done, S0 + t - 1)
                    nc.scalar.activation(hval[:, b % 2, :], bank[2 + b % 2][:, 0:T], ACT.Identity,
                                         bias=prm[:, ds(PC_B + 2 * CONF_TILES + 3 * t + 1, 1)]).then_inc(h_done, 1)
                    for s in range(5, 8):
                        hi(u + HLEAD + s, U_SC + 6 * b + HLEAD + s)
                    act.wait_ge(sc_step, 5 * t + 5)
                    nc.scalar.activation(mix_hi[:, ds(CONF_TILES + t, 1), :].rearrange("p a t -> p (a t)"), smix[:, :],
                                         ACT.Copy).then_inc(s_hi_done, 1)

            def stream_hi(first, n):
                for u in range(first, first + n):
                    hi(u, u)

            o = U_OUT + HLEAD
            stream_hi(o + 2, 7)
            act.wait_ge(cen_done, 1)
            nc.scalar.activation(cacc[:, 1, :, :], cacc[:, 0, :, :], ACT.Square).then_inc(sq_done, 1)
            stream_hi(o + 9, 3)
            act.wait_ge(veps_done, 1)
            nc.scalar.activation(lnt[:, 1, :], lnt[:, 0, :], ACT.Sqrt).then_inc(std_done, 1)
            stream_hi(o + 12, 1)
            act.wait_ge(cnorm_done, 2)
            for h in range(2):
                for t in range(4 * h, 4 * h + 4):
                    nc.scalar.activation(cacc[:, 1, t, :], cacc[:, 0, t, :], ACT.Silu,
                                         bias=prm[:, PC_LB + t:PC_LB + t + 1],
                                         scale=prm[:, PC_LG + t:PC_LG + t + 1]).then_inc(silu_done, 1)
                act.wait_ge(silu_done, 4 * h + 4)
                nc.scalar.activation(mix_hi[:, 4 * h:4 * h + 4, :], cacc[:, 1, 4 * h:4 * h + 4, :],
                                     ACT.Copy).then_inc(a_hi_done, 1)
                stream_hi(o + 13 + h, 1)
            stream_hi(o + 15, 13)
            act.wait_ge(ln_var, 1)
            nc.scalar.activation(rstd[:, 0, :], mv[:, 0, 1:2], ACT.Sqrt).then_inc(ln_std, 1)
            stream_hi(o + 28, 4)
            act.wait_ge(ln_var, 2)
            nc.scalar.activation(rstd[:, 1, :], mv[:, 1, 1:2], ACT.Sqrt).then_inc(ln_std, 1)
            for n, (b, d) in enumerate(X1_ORDER):
                act.wait_ge(x1_tr, n + 1)
                nc.scalar.activation(xt_hi[:, 4 * d:4 * d + 4, b * P:(b + 1) * P],
                                     x1_bank(b, d)[:, :].rearrange("p (k t) -> p k t", t=P), ACT.Copy)\
                    .then_inc(x1hi_done, 1)
            with act.Fori(0, HEADS // 2) as i:
                for b in range(4):
                    u = U_Q + 8 * i + 2 * b
                    t = 4 * i + b
                    hi(u + HLEAD, U_Q + 2 * b + HLEAD)
                    act.wait_ge(used, USED0 + u + 2)
                    act.wait_ge(s_ready, SC0 + t)
                    nc.scalar.activation(q_t[b % 2][:, :], bank[b % 2][:, 0:T], ACT.Copy).then_inc(qt_done, 1)
                    hi(u + HLEAD + 1, U_Q + 2 * b + HLEAD + 1)

            def gelu(c, bank_no, u_next, again=True):
                act.wait_ge(used, USED0 + u_next)
                if again:
                    act.wait_ge(clo_done, c - AHEAD * GROUP + 1)
                nc.scalar.activation(stash[:, ds(c % (AHEAD * GROUP), 1), :].rearrange("p a t -> p (a t)"),
                                     bank[bank_no][:, 0:T], ACT.Gelu).then_inc(gelu_done, 1)

            def gates_out(m, slot, t0, b):
                act.wait_ge(g_done, m + 1)
                nc.scalar.activation(gates[:, ds(slot, QUARTER), ds(t0, BATCH)].rearrange("p e t -> p t e"),
                                     bank[2 + b][:, :].rearrange("p (t w e) -> p t w e", w=2, e=QUARTER)[:, :, 0, :],
                                     ACT.Copy).then_inc(gates_up, 1)

            def coef_hi(c, r, j):
                act.wait_ge(cf_done, c + 1)
                nc.scalar.activation(c_hi[r][:, j, :],
                                     stash[:, ds(c % (AHEAD * GROUP), 1), :].rearrange("p a t -> p (a t)"),
                                     ACT.Copy).then_inc(chi_done, 1)

            for c in range(UP_FIRST):
                stream_hi(U_PRE + 2 * c + HLEAD, 1)
                if c == UP_FIRST - 1:
                    act.wait_ge(sel_tr, 1)
                    nc.scalar.activation(gate[:, :], bank[6][:, 0:T], ACT.Copy).then_inc(tabs_copied, 1)
                    nc.scalar.activation(tab2[:, :], bank[5][:, 0:T], ACT.Copy).then_inc(tabs_copied, 1)
                stream_hi(U_PRE + 2 * c + HLEAD + 1, 1)
                if c == 3:
                    act.wait_ge(rt_exp_in, 1)
                    nc.scalar.activation(sel[:, 2], sel[:, 2], ACT.Exp).then_inc(rt_exp, 1)
                gelu(c, c % 2, U_PRE + 2 * c + 2, False)
            def up_pair(i, last):
                u = U_PRE + 2 * UP_FIRST + 4 * i + HLEAD
                ur = U_PRE + 2 * UP_FIRST + HLEAD
                for n in range(4):
                    m = 4 * i + n
                    if not (last and n == 3):
                        gates_out(m, 0, BATCH * m, n % 2)
                    if last and n == 2:
                        gates_out(m + 1, 0, BATCH * (m + 1), 1)
                        for c in range(GROUP):
                            coef_hi(c, 0, c)
                    hi(u + n, ur + n)
                    if n % 2:
                        gelu(UP_FIRST + 2 * i + n // 2, n // 2, u - HLEAD + n + 1, False)

            with act.Fori(0, UP_LOOPS - 1) as i:
                up_pair(i, False)
            up_pair(UP_LOOPS - 1, True)

            def group(g, par, ups, builds):
                for j in range(GROUP):
                    if ups:
                        u, ur = U_MAIN + GSTEP * g + STEP * j, U_MAIN + STEP * j
                    else:
                        u, ur = U_TAIL + 2 * GROUP * (g - GROUPS + AHEAD) + 2 * j, U_TAIL + 2 * j
                    if not (isinstance(g, int) and g == GROUPS - 1):
                        coef_hi(GROUP * (g + 1) + j, (par + 1) % 2, j)
                    n = STEP if ups else 2
                    for s in range(n):
                        if s == n - 1 and builds:
                            for m, _, slot, t0, r in batches(g, j):
                                gates_out(m, slot, t0, r)
                        if not (isinstance(u, int) and u + HLEAD + s >= U_END):
                            hi(u + HLEAD + s, ur + HLEAD + s)
                    if ups:
                        gelu(GROUP * (g + AHEAD) + j, j % 2, u + STEP)

            group(0, 0, True, True)
            with act.Fori(0, 11) as p:
                for b in range(2):
                    group(2 * p + 1 + b, 1 + b, True, True)
            for g in range(23, GROUPS - AHEAD):
                group(g, g % 2, True, False)
            with act.Fori((GROUPS - AHEAD) // 2, GROUPS // 2 - 1) as p:
                for b in range(2):
                    group(2 * p + b, b, False, False)
            for g in range(GROUPS - 2, GROUPS):
                group(g, g % 2, False, False)

            n_normed = 0
            for b in range(TB):
                act.wait_ge(ln_var, TB + b + 1)
                nc.scalar.activation(rstd[:, b, :], mv[:, b, 1:2], ACT.Sqrt).then_inc(ln_std, 1)
                nc.scalar.activation(neg_mean[:, b, :], mv[:, b, 0:1], ACT.Copy, scale=-1.0).then_inc(neg_done, 1)
                act.wait_ge(neg_done, b + 1)
                mine = [d for block, d in LN2_POOL if block == b]
                for d in mine:
                    nc.scalar.activation(acc[:, b, d * DCH:(d + 1) * DCH], acc[:, b, d * DCH:(d + 1) * DCH],
                                         ACT.Identity, bias=neg_mean[:, b, :]).then_inc(normed, 1)
                    n_normed += 1
                    act.wait_ge(ln2_rstd, b + 1)
                    act.wait_ge(normed, n_normed)
                    nc.scalar.activation(acc[:, b, d * DCH:(d + 1) * DCH], acc[:, b, d * DCH:(d + 1) * DCH],
                                         ACT.Copy, scale=rstd[:, b, :]).then_inc(normed, 1)
                    n_normed += 1
            for n, (b, d) in enumerate(LN2_POOL):
                act.wait_ge(fin_pool, n + 1)
                act.dma_start(out[b * P:(b + 1) * P, d * DCH:(d + 1) * DCH],
                              acc[:, b, d * DCH:(d + 1) * DCH]).then_inc(out_done, 16)

        @block.vector
        def _(dve):
            tt = nc.vector.tensor_tensor
            ts = nc.vector.tensor_scalar
            stt = nc.vector.scalar_tensor_tensor

            def lo(u, slot_u):
                if vector_takes(slot_u):
                    dve.wait_ge(hi_done, u + 1)
                    tt(w_lo[slot_u % SPLIT][:, :], raw[:, slot_u % RAW, :], w_hi[slot_u % SPLIT][:, :].bitcast(f32),
                       ALU.subtract).then_inc(lo_done[slot_u % SPLIT], SPLIT)

            def stream_lo(first, n):
                for u in range(first, first + n):
                    lo(u, u)

            credits = ((used, USED0), (glu_done, GLU0), (s_done, S0), (taps_done, TAPS0), (s_ready, SC0),
                       (gates_done, GATES0))
            for n, (credit, count) in enumerate(credits):
                nc.vector.memset(stats[:, 0, 0, n:n + 1], 0.0).then_inc(credit, count)

            def x_lo(c):
                dve.wait_ge(xhi_done, c + 1)
                tt(xt_lo[:, 4 * c:4 * c + 4, :], xt_raw[:, 4 * c:4 * c + 4, :],
                   xt_hi[:, 4 * c:4 * c + 4, :].bitcast(f32), ALU.subtract).then_inc(xlo_done, 1)

            lo(0, 0)
            for c in range(4):
                x_lo(c)
            lo(2, 2)
            dve.wait_ge(prm_in, 16)
            dve.wait_ge(pool_done, 5)

            def tap(t, k, first_wait):
                a = apad[:, ds(t, 1), k:k + T]
                w = prm[:, ds(PC_CW + TAPS * t + k, 1)]
                s = cacc[:, k % 2, ds(t, 1), :]
                dve.wait_ge(taps_done, TAPS0 + first_wait)
                if k == 0:
                    i = ts(s, a, w, prm[:, ds(PC_CB + t, 1)], ALU.mult, ALU.add)
                elif k == 1:
                    i = ts(s, a, w, None, ALU.mult)
                else:
                    i = stt(s, a, w, s, ALU.mult, ALU.add)
                i.then_inc(taps_done, 1)

            chain = [0]

            def link(ins):
                chain[0] += 1
                ins.then_inc(ln_chain, 1)
                return chain[0]

            def chunk(b, d):
                return acc[:, b, d * DCH:(d + 1) * DCH]

            def add_chunk(b, d, psum):
                return link(tt(chunk(b, d), psum[:, :], chunk(b, d), ALU.add))

            def chunk_stats(b, d, added):
                dve.wait_ge(ln_chain, added)
                return link(nc.vector.bn_stats(stats[:, b, d, :], chunk(b, d)))

            def moments(b):
                dve.wait_ge(ln_chain, chain[0])
                dve.wait_ge(ln_chain, link(nc.vector.bn_aggr(mv[:, b, :],
                                                             stats[:, b, :, :].rearrange("p c s -> p (c s)"))))
                nc.vector.tensor_scalar_add(mv[:, b, 1:2], mv[:, b, 1:2], EPS).then_inc(ln_var, 1)

            def inverse(b, count):
                dve.wait_ge(ln_std, count)
                return link(nc.vector.reciprocal(rstd[:, b, :], rstd[:, b, :]))

            def centre(b, d, g):
                return link(stt(chunk(b, d), chunk(b, d), mv[:, b, 0:1], g[:, d * DCH:(d + 1) * DCH],
                                ALU.subtract, ALU.mult))

            def scale(b, d, b_, needs, done):
                dve.wait_ge(ln_chain, needs)
                stt(chunk(b, d), chunk(b, d), rstd[:, b, :], b_[:, d * DCH:(d + 1) * DCH],
                    ALU.mult, ALU.add).then_inc(done, 1)

            def x1_lo(n):
                b, d = X1_ORDER[n]
                dve.wait_ge(x1hi_done, n + 1)
                tt(xt_lo[:, 4 * d:4 * d + 4, b * P:(b + 1) * P], x1_bank(b, d)[:, :].rearrange("p (k t) -> p k t", t=P),
                   xt_hi[:, 4 * d:4 * d + 4, b * P:(b + 1) * P].bitcast(f32), ALU.subtract).then_inc(x1lo_done, 1)

            H1 = 14
            stream_lo(U_CONF + LEAD, 4)
            with dve.Fori(0, CONF_TILES // 2) as i:
                for b in range(2):
                    u = U_CONF + 8 * i + 4 * (b + 1) + LEAD
                    t = 2 * i + b
                    dve.wait_ge(sig_done, t + 1)
                    stt(apad[:, ds(t, 1), TAPS - 1:TAPS - 1 + T].rearrange("p a t -> p (a t)"), bank[b][:, 0:T],
                        prm[:, ds(PC_B + 2 * t, 1)], sig[:, b, :], ALU.add, ALU.mult).then_inc(glu_done, 1)
                    dve.wait_ge(glu_done, GLU0 + t + 1)
                    for s in range(4):
                        for k in range(H1 * s // 4, H1 * (s + 1) // 4):
                            tap(t, k, H1 * t + max(k - 1, 0))
                        lo(u + s, U_CONF + 4 * (b + 1) + LEAD + s)
            dve.wait_ge(xn_in, 16)
            dve.wait_ge(bo_in, 16)
            for b in range(TB):
                stt(acc[:, b, :], acc[:, b, :], ALPHA, bo[:, :], ALU.mult, ALU.add).then_inc(xres_done, 1)
                stream_lo(U_SC + LEAD + 4 + b, 1)
            T1 = H1 * CONF_TILES
            H2 = TAPS - H1
            LO_AT = (1, 4, 7, 10, 13, H2 - 1)
            MIX_AT = 9
            with dve.Fori(0, SC_TILES // 4) as i:
                for b in range(4):
                    u = U_SC + 24 * i + 6 * (b + 1) + LEAD
                    t = 4 * i + b
                    col = PC_B + 2 * CONF_TILES + 3 * t

                    def short_conv(step):
                        if step == 0:
                            return stt(scpad[:, 2:2 + T], bank[b % 2][:, 0:T], prm[:, ds(col, 1)], hval[:, b % 2, :],
                                       ALU.add, ALU.mult)
                        if step == 1:
                            return ts(sct[:, 0, :], scpad[:, 0:T], prm[:, ds(PC_SW + 3 * t, 1)],
                                      prm[:, ds(PC_SB + t, 1)], ALU.mult, ALU.add)
                        if step < 4:
                            tap_no = step - 1
                            return stt(sct[:, (step + 1) % 2, :], scpad[:, tap_no:tap_no + T],
                                       prm[:, ds(PC_SW + 3 * t + tap_no, 1)], sct[:, step % 2, :], ALU.mult, ALU.add)
                        return stt(smix[:, :], bank[4 + b % 2][:, 0:T], prm[:, ds(col + 2, 1)], sct[:, 0, :],
                                   ALU.add, ALU.mult)

                    dve.wait_ge(h_done, t + 1)
                    for k in range(H2):
                        if k < 5:
                            if k:
                                dve.wait_ge(sc_step, 5 * t + k)
                            short_conv(k).then_inc(sc_step, 1)
                        tap(t, H1 + k, T1 + H2 * t + max(k - 1, 0))
                        if k in LO_AT:
                            s = LO_AT.index(k)
                            lo(u + s, U_SC + 6 * (b + 1) + LEAD + s)
                        if k == MIX_AT:
                            dve.wait_ge(s_hi_done, t + 1)
                            tt(mix_lo[:, ds(CONF_TILES + t, 1), :].rearrange("p a t -> p (a t)"), smix[:, :],
                               mix_hi[:, ds(CONF_TILES + t, 1), :].bitcast(f32).rearrange("p a t -> p (a t)"),
                               ALU.subtract).then_inc(s_done, 1)
            o = U_OUT + LEAD
            dve.wait_ge(taps_done, TAPS0 + T1 + H2 * CONF_TILES)
            tt(cacc[:, 0, :, :], cacc[:, 0, :, :], cacc[:, 1, :, :], ALU.add).then_inc(cconv_done, 1)
            dve.wait_ge(cconv_done, 1)

            def sum_tiles(src, done):
                n = CONF_TILES // 2
                tt(cacc[:, 1, 0:n, :], cacc[:, src, 0:n, :], cacc[:, src, n:2 * n, :], ALU.add).then_inc(done, 1)
                for k in range(1, 3):
                    n //= 2
                    dve.wait_ge(done, k)
                    tt(cacc[:, 1, 0:n, :], cacc[:, 1, 0:n, :], cacc[:, 1, n:2 * n, :], ALU.add).then_inc(done, 1)

            sum_tiles(0, csum_done)
            stream_lo(o + 6, 3)
            dve.wait_ge(mean_done, 1)
            tt(cacc[:, 0, :, :], cacc[:, 0, :, :], bank[0][:, 0:T].unsqueeze(1).to_broadcast([P, CONF_TILES, T]),
               ALU.subtract).then_inc(cen_done, 1)
            dve.wait_ge(sq_done, 1)
            sum_tiles(1, sqsum_done)
            stream_lo(o + 9, 3)
            dve.wait_ge(var_done, 1)
            nc.vector.tensor_scalar_add(lnt[:, 0, :], bank[2][:, 0:T], EPS).then_inc(veps_done, 1)
            stream_lo(o + 12, 1)
            dve.wait_ge(std_done, 1)
            nc.vector.reciprocal(lnt[:, 0, :], lnt[:, 1, :]).then_inc(veps_done, 1)
            dve.wait_ge(veps_done, 2)
            for h in range(2):
                sl = slice(4 * h, 4 * h + 4)
                tt(cacc[:, 0, sl, :], cacc[:, 0, sl, :], lnt[:, 0, :].unsqueeze(1).to_broadcast([P, 4, T]),
                   ALU.mult).then_inc(cnorm_done, 1)
            stream_lo(o + 13, 1)
            for h in range(2):
                dve.wait_ge(a_hi_done, h + 1)
                tt(mix_lo[:, 4 * h:4 * h + 4, :], cacc[:, 1, 4 * h:4 * h + 4, :],
                   mix_hi[:, 4 * h:4 * h + 4, :].bitcast(f32), ALU.subtract).then_inc(a_lo_done, 1)
                stream_lo(o + 14 + h, 1)

            lo_next = o + 16
            dve.wait_ge(xres_done, 2)
            for d in range(NCH - 1):
                stream_lo(lo_next, o + 21 + 4 * d - lo_next)
                lo_next = o + 21 + 4 * d
                dve.wait_ge(used, USED0 + U_OUT + 4 * (NCH + d + 1))
                added = [add_chunk(b, d, y_banks[d][b]) for b in range(TB)]
                for b in range(TB):
                    chunk_stats(b, d, added[b])
            stream_lo(lo_next, U_Q + LEAD - lo_next)
            d = NCH - 1
            dve.wait_ge(y0_done, 1)
            chunk_stats(0, d, add_chunk(0, d, y_banks[d][0]))
            moments(0)
            dve.wait_ge(ln1_in, 32)
            centre(0, 0, ln_g)
            inverse(0, 1)
            c01 = centre(0, 1, ln_g)
            scale(0, 0, ln_b, c01 - 1, x1_done)
            c02 = centre(0, 2, ln_g)
            scale(0, 1, ln_b, c01, x1_done)
            scale(0, 2, ln_b, c02, x1_done)
            dve.wait_ge(used, USED0 + U_Q)
            chunk_stats(1, d, add_chunk(1, d, y_banks[d][1]))
            moments(1)
            centre(1, 0, ln_g)
            inverse(1, 2)
            c11 = centre(1, 1, ln_g)
            scale(1, 0, ln_b, c11 - 1, x1_done)
            c03 = centre(0, 3, ln_g)
            scale(1, 1, ln_b, c11, x1_done)
            for n in range(X1_HALF):
                x1_lo(n)
            c12 = centre(1, 2, ln_g)
            scale(0, 3, ln_b, c03, x1_done)
            c13 = centre(1, 3, ln_g)
            scale(1, 2, ln_b, c12, x1_done)
            scale(1, 3, ln_b, c13, x1_done)
            for n in range(X1_HALF, TB * NCH):
                x1_lo(n)
            dve.wait_ge(x1_tr, 8)
            nc.vector.tensor_scalar_mul(acc[:, :, :], acc[:, :, :], ALPHA).then_inc(xres_done, 1)

            NEG = -3.0e38

            def top16(src, rest, v, idx, first):
                steps = [
                    lambda b: nc.vector.max(v(b, 0), src(b)),
                    lambda b: nc.vector.max_index(idx(b, 0), v(b, 0), src(b)),
                    lambda b: nc.vector.match_replace(rest(b), v(b, 0), src(b), NEG),
                    lambda b: nc.vector.max(v(b, 1), rest(b)),
                    lambda b: nc.vector.max_index(idx(b, 1), v(b, 1), rest(b)),
                ]
                needs = [None, 0, 0, 2, 3]
                for n, step in enumerate(steps):
                    for b in range(TB):
                        if needs[n] is not None:
                            dve.wait_ge(rt, first + 2 * needs[n] + b + 1)
                            dve.nop(nofuse=True)
                        step(b).then_inc(rt, 1)

            dve.wait_ge(iota_done, 2)
            dve.wait_ge(x1lo_done, 8)
            stream_lo(U_Q + LEAD, 6 - LEAD)
            nc.vector.tensor_copy(iota16[:, :, :], iota[:, 0:TOPK].unsqueeze(2).to_broadcast([P, TOPK, TOPK]))\
                .then_inc(iota_done, 1)
            nc.vector.memset(ssum[:, :, :], 0.0).then_inc(rt, PER_HEAD)
            with dve.Fori(0, HEADS // 2) as i:
                for b4 in range(4):
                    t = 4 * i + b4
                    h = 2 * i + b4 // 2
                    r0 = PER_HEAD * (h + 1) + 11 * (b4 % 2)
                    dve.wait_ge(s_ready, SC0 + t + 1)
                    dve.nop(nofuse=True)
                    top16(lambda b: bank[2 + b4 % 2][:, b * P:(b + 1) * P],
                          lambda b: srest[:, b, :],
                          lambda b, e: hv[b4 % 2][:, b, 8 * e:8 * e + 8],
                          lambda b, e: hidx[b4 % 2][:, b, 8 * e:8 * e + 8], r0)
                    lo(U_Q + 8 * i + 2 * b4 + 6, U_Q + 2 * b4 + 6)
                    dve.wait_ge(rt, r0 + 10)
                    nc.vector.tensor_copy(hidx_f[:, :, ds(t, 1), :].rearrange("p b a k -> p b (a k)"),
                                          hidx[b4 % 2][:, :, :]).then_inc(rt, 1)
                    if b4 % 2:
                        r1 = PER_HEAD * (h + 1) + 22
                        dve.wait_ge(rt, r1)
                        for b in range(TB):
                            tt(cand[:, b, :, :],
                               hv[0][:, b, :].unsqueeze(2).to_broadcast([P, TOPK, TOPK]),
                               hv[1][:, b, :].unsqueeze(1).to_broadcast([P, TOPK, TOPK]), ALU.add).then_inc(rt, 1)
                        dve.wait_ge(rt, r1 + 2)
                        dve.nop(nofuse=True)
                        top16(lambda b: cand[:, b, :, :].rearrange("p a k -> p (a k)"),
                              lambda b: crest[:, b, :],
                              lambda b, e: cv[:, b, 8 * e:8 * e + 8],
                              lambda b, e: cidx[:, b, 8 * e:8 * e + 8], r1 + 2)
                        dve.wait_ge(rt, r1 + 12)
                        nc.vector.tensor_copy(tv[:, :, ds(h, 1), :].rearrange("p b a k -> p b (a k)"),
                                              cv[:, :, :]).then_inc(rt, 1)
                        nc.vector.tensor_copy(tci[:, :, ds(h, 1), :].rearrange("p b a k -> p b (a k)"),
                                              cidx[:, :, :]).then_inc(rt, 1)
            R = [PER_HEAD * (HEADS + 1)]

            def link_rt(ins):
                R[0] += 1
                ins.then_inc(rt, 1)

            lo_units = [u for u in range(U_PRE + 5, U_PRE + 2 * UP_FIRST + LEAD) if vector_takes(u)]

            def lo_next_unit():
                u = lo_units.pop(0)
                lo(u, u)

            dve.wait_ge(rt, R[0])
            tt(sel[:, 2], tv[:, :, :, :], tv[:, :, :, 0:1].to_broadcast([P, TB, HEADS, TOPK]),
               ALU.subtract).then_inc(rt_exp_in, 1)
            link_rt(nc.vector.tensor_single_scalar(tab_u[:, 0], tci[:, :, :, :], 4, ALU.logical_shift_right))
            link_rt(nc.vector.tensor_single_scalar(tab_u[:, 1], tci[:, :, :, :], 15, ALU.bitwise_and))
            dve.wait_ge(rt, R[0])
            link_rt(nc.vector.tensor_copy(tab_f[:, :, :, :, :], tab_u[:, :, :, :, :]))
            dve.wait_ge(rt, R[0])
            dve.wait_ge(iota_done, 3)
            decodes = [(half, b) for half in range(2) for b in range(TB)]

            def matches(n):
                half, b = decodes[n]
                link_rt(tt(eq[n % 2][:, :, :, :], tab_f[:, half, b].unsqueeze(2).to_broadcast([P, HEADS, TOPK, TOPK]),
                        iota16[:, :, :].unsqueeze(1).to_broadcast([P, HEADS, TOPK, TOPK]), ALU.is_equal))

            matches(0)
            for n, (half, b) in enumerate(decodes):
                e = eq[n % 2]
                mine = hidx_f[:, b, :, :].rearrange("p (h two) k -> p h two k", two=2)[:, :, half, :]
                dve.wait_ge(rt, R[0])
                link_rt(tt(e[:, :, :, :], e[:, :, :, :], mine.unsqueeze(3).to_broadcast([P, HEADS, TOPK, TOPK]),
                        ALU.mult))
                if n % 2 == 0:
                    lo_next_unit()
                product = R[0]
                if n + 1 < len(decodes):
                    matches(n + 1)
                dve.wait_ge(rt, product)
                link_rt(tt(e[:, :, 0:8, :], e[:, :, 0:8, :], e[:, :, 8:16, :], ALU.add))
                dve.wait_ge(rt, R[0])
                link_rt(tt(e[:, :, 0:4, :], e[:, :, 0:4, :], e[:, :, 4:8, :], ALU.add))
                dve.wait_ge(rt, R[0])
                link_rt(nc.vector.tensor_reduce(sel[:, half, b], e[:, :, 0:4, :].rearrange("p h j k -> p h k j"),
                                                AX.X, ALU.add))
            dve.wait_ge(rt_exp, 1)
            link_rt(nc.vector.tensor_reduce(ssum[:, :, :], sel[:, 2], AX.X, ALU.add))
            dve.wait_ge(rt, R[0])
            link_rt(nc.vector.reciprocal(ssum[:, :, :], ssum[:, :, :]))
            lo_next_unit()
            dve.wait_ge(rt, R[0])
            tt(sel[:, 2], sel[:, 2], ssum[:, :, :].unsqueeze(3).to_broadcast([P, TB, HEADS, TOPK]),
               ALU.mult).then_inc(sel_done, 1)
            dve.wait_ge(sel_tr, 1)
            nc.vector.tensor_copy(tab1[:, :], bank[4][:, 0:T]).then_inc(tabs_done, 1)
            dve.wait_ge(tabs_copied, 1)
            nc.vector.tensor_single_scalar(gate_e[:, :], gate[:, :].bitcast(u32), EXPONENT,
                                           ALU.bitwise_and).then_inc(tabs_done, 1)
            ts(gate_m[:, :], gate[:, :].bitcast(u32), FRACTION, ONE, ALU.bitwise_and,
               ALU.bitwise_or).then_inc(tabs_done, 1)
            dve.wait_ge(tabs_done, 3)
            nc.vector.tensor_copy(gate_p[:, :], gate_e[:, :].bitcast(f32)).then_inc(tabs_done, 1)
            nc.vector.tensor_copy(gate_t[:, 0, :], gate_m[:, :].bitcast(f32)).then_inc(tabs_done, 1)
            dve.wait_ge(tabs_done, 5)
            tt(gate_r[:, :], gate_m[:, :].bitcast(f32), gate_t[:, 0, :], ALU.subtract).then_inc(tabs_done, 1)
            dve.wait_ge(tabs_done, 6)
            nc.vector.tensor_scalar_mul(gate_t[:, 1, :], gate_r[:, :], LOWER).then_inc(tabs_done, 1)
            dve.wait_ge(tabs_done, 7)
            dve.wait_ge(tabs_copied, 2)

            def onehot2(m, key0, t0):
                if not (isinstance(m, int) and m == 0):
                    dve.wait_ge(oh_chain, m)
                tt(oh2[:, :, :], iota_t[:, ds(key0, QUARTER), :],
                   tab2[:, ds(t0, BATCH)].unsqueeze(1).to_broadcast([P, QUARTER, BATCH]), ALU.is_equal)\
                    .then_inc(oh_first, 1)

            def onehot1(m, t0, b):
                if not (isinstance(m, int) and m < 2):
                    dve.wait_ge(g_done, m - 1)
                tt(oh1[b][:, :, :], iota_t[:, :, :],
                   tab1[:, ds(t0, BATCH)].unsqueeze(1).to_broadcast([P, P, BATCH]), ALU.is_equal).then_inc(oh1_first, 1)

            def gated(m, t0, b):
                dve.wait_ge(oh1_first, m + 1)
                tt(oh1[b][:, :, :], oh1[b][:, :, :],
                   gate_p[:, ds(t0, BATCH)].unsqueeze(1).to_broadcast([P, P, BATCH]), ALU.mult).then_inc(oh_done, 1)
                dve.wait_ge(oh_first, m + 1)
                tt(oh2g[b][:, :, :, :], oh2[:, :, :].unsqueeze(1).to_broadcast([P, PARTS, QUARTER, BATCH]),
                   gate_t[:, :, ds(t0, BATCH)].unsqueeze(2).to_broadcast([P, PARTS, QUARTER, BATCH]),
                   ALU.mult).then_inc(oh_chain, 1)

            def build(m, key0, t0, b):
                onehot2(m, key0, t0)
                onehot1(m, t0, b)
                gated(m, t0, b)

            def gates_add(m, slot, t0, b):
                dve.wait_ge(gates_up, m + 1)
                sl = gates[:, ds(slot, QUARTER), ds(t0, BATCH)].rearrange("p e t -> p t e")
                stt(sl, bank[2 + b][:, :].rearrange("p (t w e) -> p t w e", w=2, e=QUARTER)[:, :, 1, :],
                    1.0 / LOWER, sl, ALU.mult, ALU.add).then_inc(gates_done, 1)

            build(0, 0, 0, 0)
            while lo_units:
                lo_next_unit()
            build(1, 0, BATCH, 1)

            def stashed(c):
                return stash[:, ds(c % (AHEAD * GROUP), 1), :].rearrange("p a t -> p (a t)")

            def coef(c, slot, gates_needed):
                dve.wait_ge(gelu_done, c + 1)
                dve.wait_ge(gates_done, GATES0 + gates_needed)
                tt(stashed(c), stashed(c), gates[:, ds(slot, 1), :].rearrange("p a t -> p (a t)"),
                   ALU.mult).then_inc(cf_done, 1)

            def coef_lo(c, r, j):
                dve.wait_ge(chi_done, c + 1)
                tt(c_lo[r][:, j, :], stashed(c), c_hi[r][:, j, :].bitcast(f32), ALU.subtract).then_inc(clo_done, 1)

            def first_coefficients():
                for c in range(0, GROUP, 2):
                    for n in range(c, c + 2):
                        coef(n, n, T // BATCH)
                    for n in range(c, c + 2):
                        coef_lo(n, 0, n)

            def up_pair(i, last):
                u = U_PRE + 2 * UP_FIRST + 4 * i + LEAD
                ur = U_PRE + 2 * UP_FIRST + LEAD
                for n in range(2 if last else 4):
                    m = 4 * i + n
                    gates_add(m, 0, BATCH * m, n % 2)
                    build(m + 2, 0, BATCH * (m + 2), n % 2)
                    lo(u + n, ur + n)
                if last:
                    for n in range(2, 4):
                        gates_add(4 * i + n, 0, BATCH * (4 * i + n), n % 2)
                    first_coefficients()
                    for n in range(2, 4):
                        lo(u + n, ur + n)

            with dve.Fori(0, UP_LOOPS - 1) as i:
                up_pair(i, False)
            up_pair(UP_LOOPS - 1, True)

            dve.wait_ge(xres_done, 3)
            for n in range(2):
                build(T // BATCH + n, QUARTER, BATCH * n, n)

            def add_v(u_next, c, b2):
                dve.wait_ge(used, USED0 + u_next)
                for b in range(TB):
                    sl = acc[:, b, c * DCH:(c + 1) * DCH]
                    i = tt(sl, bank[4 + 2 * (b2 % 2) + b][:, :], sl, ALU.add)
                i.then_inc(acc_done, 1)

            def group(g, par, ups, builds):
                g_last = isinstance(g, int) and g == GROUPS - 1
                more = not g_last
                for j in range(GROUP):
                    if ups:
                        u, ur = U_MAIN + GSTEP * g + STEP * j, U_MAIN + STEP * j
                    else:
                        u, ur = U_TAIL + 2 * GROUP * (g - GROUPS + AHEAD) + 2 * j, U_TAIL + 2 * j
                    c = GROUP * (g + 1) + j
                    turn = list(batches(g, j)) if builds else []
                    if isinstance(g, int) and g == 0:
                        coef(c, GROUP + j, T // BATCH)
                        lo(u + LEAD, ur + LEAD)
                        coef_lo(c, 1, j)
                        for s in range(1, 3):
                            lo(u + LEAD + s, ur + LEAD + s)
                        add_v(u + 2, j, j)
                        for m, key0, slot, t0, r in turn:
                            gates_add(m, slot, t0, r)
                            if m + 2 < 2 * GROUP + T // BATCH:
                                build(m + 2, key0, t0 + 2 * BATCH, r)
                        lo(u + LEAD + 3, ur + LEAD + 3)
                        continue
                    m, key0, slot, t0, r = turn[0] if builds else (None,) * 5

                    def split(s):
                        if not (isinstance(u, int) and u + LEAD + s >= U_END):
                            lo(u + LEAD + s, ur + LEAD + s)

                    if more:
                        coef(c, GROUP * ((g + 1) % (2 * GROUPS_Q)) + j, (T // BATCH) * ((g + 1) // GROUPS_Q + 1))
                    if builds:
                        onehot2(m, key0, t0)
                    split(0)
                    if more:
                        coef_lo(c, (par + 1) % 2, j)
                    if builds:
                        onehot1(m, t0, j % 2)
                    split(1)
                    if builds:
                        gated(m, t0, j % 2)
                    if ups:
                        split(2)
                    if g_last and j == GROUP - 1:
                        dve.wait_ge(v0_done, 1)
                        chunk_stats(0, j, add_chunk(0, j, bank[4 + 2 * (j % 2)]))
                        continue
                    add_v(u + 2, j, j)
                    if g_last:
                        dve.wait_ge(acc_done, GROUP * g + j + 1)
                        for b in range(TB):
                            chunk_stats(b, j, chain[0])
                    if ups:
                        split(3)
                    if builds:
                        gates_add(m, slot, t0, j % 2)

            group(0, 0, True, True)
            with dve.Fori(0, 11) as p:
                for b in range(2):
                    group(2 * p + 1 + b, 1 + b, True, True)
            for g in range(23, GROUPS - AHEAD):
                group(g, g % 2, True, False)
            with dve.Fori((GROUPS - AHEAD) // 2, GROUPS // 2 - 1) as p:
                for b in range(2):
                    group(2 * p + b, b, False, False)
            for g in range(GROUPS - 2, GROUPS):
                group(g, g % 2, False, False)
            moments(0)
            dve.wait_ge(ln2_in, 32)
            centre(0, 0, ln2g)
            inverse(0, TB + 1)
            dve.wait_ge(ln_chain, chain[0])
            nc.vector.memset(stats[:, 0, 0, 0:1], 0.0).then_inc(ln2_rstd, 1)
            scale(0, 0, ln2b, chain[0], fin)
            dve.wait_ge(used, USED0 + U_END)
            d = NCH - 1
            chunk_stats(1, d, add_chunk(1, d, bank[4 + 2 * (d % 2) + 1]))
            moments(1)
            c01 = centre(0, 1, ln2g)
            inverse(1, TB + 2)
            dve.wait_ge(ln_chain, chain[0])
            nc.vector.memset(stats[:, 0, 0, 0:1], 0.0).then_inc(ln2_rstd, 1)
            c10 = centre(1, 0, ln2g)
            scale(0, 1, ln2b, c01, fin)
            c11 = centre(1, 1, ln2g)
            scale(1, 0, ln2b, c10, fin)
            c12 = centre(1, 2, ln2g)
            scale(1, 1, ln2b, c11, fin)
            scale(1, 2, ln2b, c12, fin)

        @block.tensor
        def _(pe):
            mm = nc.tensor.matmul

            def stationary_unit(u, slot_u, half, dst, x_ready=None):
                wait_lo(pe, u, slot_u)
                hi_w, lo_w = w_hi[slot_u % SPLIT], w_lo[slot_u % SPLIT]
                for k in range(HALF):
                    kk = HALF * half + k
                    if x_ready and k % 4 == 0:
                        pe.wait_ge(x_ready, kk // 4 + 1)
                    sl = slice(k * P, (k + 1) * P)
                    st, en = half == 0 and k == 0, half == 1 and k == HALF - 1
                    mm(dst, hi_w[:, sl], xt_hi[:, kk, :], start=st, stop=False)
                    mm(dst, hi_w[:, sl], xt_lo[:, kk, :], start=False, stop=False)
                    i = mm(dst, lo_w[:, sl], xt_hi[:, kk, :], start=False, stop=en)
                i.then_inc(used, 1)

            with pe.Fori(0, CONF_TILES // 2) as i:
                for b in range(2):
                    t = 2 * i + b
                    pe.wait_ge(glu_done, GLU0 + t - 1)
                    for w in range(2):
                        for h in range(2):
                            n = 4 * b + 2 * w + h
                            stationary_unit(U_CONF + 8 * i + n, U_CONF + n, h, bank[2 * w + b][:, 0:T], xlo_done)
            with pe.Fori(0, SC_TILES // 4) as i:
                for b in range(4):
                    t = 4 * i + b
                    if b < 2:
                        pe.wait_ge(glu_done, GLU0 + CONF_TILES - 1 + b)
                    pe.wait_ge(s_done, S0 + t - 1)
                    for w in range(3):
                        for h in range(2):
                            n = 6 * b + 2 * w + h
                            stationary_unit(U_SC + 24 * i + n, U_SC + n, h, bank[2 * w + b % 2][:, 0:T])

            def out_units(u0, k0, d, first, last):
                whole = not (last and d == NCH - 1)
                for n, blocks in [(n, [0, 1]) for n in range(4)] if whole else [(n, [b]) for b in (0, 1) for n in range(4)]:
                    wait_lo(pe, u0 + n, u0 + n)
                    hi_w, lo_w = w_hi[(u0 + n) % SPLIT], w_lo[(u0 + n) % SPLIT]
                    for k in range(2):
                        kk = k0 + 2 * n + k
                        if u0 < U_OUT + 4:
                            pe.wait_ge(s_done, S0 + kk - CONF_TILES + 1)
                        if u0 == U_OUT + 4 * NCH and k == 0:
                            pe.wait_ge(a_lo_done, n // 2 + 1)
                        st, en = first and n == 0 and k == 0, last and n == 3 and k == 1
                        w1, w2 = hi_w[:, k * DCH:(k + 1) * DCH], lo_w[:, k * DCH:(k + 1) * DCH]
                        for b in blocks:
                            a1, a2 = mix_hi[:, kk, b * P:(b + 1) * P], mix_lo[:, kk, b * P:(b + 1) * P]
                            dst = y_banks[d][b][:, :]
                            mm(dst, a1, w1, start=st, stop=False)
                            mm(dst, a1, w2, start=False, stop=False)
                            i = mm(dst, a2, w1, start=False, stop=en)
                    if 1 in blocks:
                        i.then_inc(used, 1)
                    elif n == 3:
                        i.then_inc(y0_done, 1)

            for d in range(2):
                out_units(U_OUT + 4 * d, CONF_TILES, d, True, False)
            pe.wait_ge(csum_done, 3)
            mm(bank[0][:, 0:T], ones[:, :], cacc[:, 1, 0, :], start=True, stop=True).then_inc(mean_done, 1)
            out_units(U_OUT + 8, CONF_TILES, 2, True, False)
            pe.wait_ge(sqsum_done, 3)
            mm(bank[2][:, 0:T], ones[:, :], cacc[:, 1, 0, :], start=True, stop=True).then_inc(var_done, 1)
            pe.wait_ge(veps_done, 1)
            out_units(U_OUT + 12, CONF_TILES, 3, True, False)
            for d in range(NCH):
                out_units(U_OUT + 16 + 4 * d, 0, d, False, True)
            pe.wait_ge(pool_done, 5)
            def transpose_x1(n):
                b, d = X1_ORDER[n]
                pe.wait_ge(x1_done, n + 1)
                for k in range(4):
                    i = nc.tensor.transpose(x1_bank(b, d)[:, k * P:(k + 1) * P],
                                            acc[:, b, d * DCH + k * P:d * DCH + (k + 1) * P], ident[:, :])
                i.then_inc(x1_tr, 1)

            for n in range(X1_HALF):
                transpose_x1(n)
            pe.wait_ge(keys_in, 16)

            def scores(t, b4, h_pair):
                pe.wait_ge(qt_done, t + 1)
                pe.wait_ge(rt, PER_HEAD * (2 * h_pair + b4 // 2) + 11 * (b4 % 2) + 6)
                for b in range(TB):
                    i = mm(bank[2 + b4 % 2][:, b * P:(b + 1) * P], q_t[b4 % 2][:, b * P:(b + 1) * P],
                           keys[:, ds(N_KEYS * t, N_KEYS)], start=True, stop=True)
                i.then_inc(s_ready, 1)

            def q_tiles(i, last):
                for b4 in range(4):
                    n = 2 * b4
                    stationary_unit(U_Q + 8 * i + n + 1, U_Q + n + 1, 1, bank[b4 % 2][:, 0:T])
                    if not (last and b4 == 3):
                        stationary_unit(U_Q + 8 * i + n + 2, U_Q + n + 2, 0, bank[(b4 + 1) % 2][:, 0:T])
                    scores(4 * i + b4, b4, i)

            pe.wait_ge(x1lo_done, X1_HALF)
            stationary_unit(U_Q, U_Q, 0, bank[0][:, 0:T])
            for n in range(X1_HALF, TB * NCH):
                transpose_x1(n)
            pe.wait_ge(x1lo_done, 8)
            with pe.Fori(0, HEADS // 2 - 1) as i:
                q_tiles(i, False)
            q_tiles(HEADS // 2 - 1, True)

            def up(c, c_ring, u, ur, between=None):
                if not (isinstance(c, int) and c < 2):
                    pe.wait_ge(gelu_done, c - 1)
                for h in range(2):
                    stationary_unit(u + h, ur + h, h, bank[c_ring % 2][:, 0:T])
                    if h == 0 and between:
                        between()

            def transpose_selections():
                pe.wait_ge(sel_done, 1)
                for w in range(3):
                    for b in range(TB):
                        i = nc.tensor.transpose(bank[4 + w][:, b * P:(b + 1) * P],
                                                sel[:, w, b].rearrange("p h k -> p (h k)"), ident[:, :])
                i.then_inc(sel_tr, 1)

            for c in range(UP_FIRST):
                up(c, c, U_PRE + 2 * c, U_PRE + 2 * c, transpose_selections if c == UP_FIRST - 1 else None)

            def gate_batch(m, b):
                pe.wait_ge(oh_done, m + 1)
                pe.wait_ge(oh_chain, m + 1)
                if not (isinstance(m, int) and m < 2):
                    pe.wait_ge(gates_done, GATES0 + m - 1)
                for t in range(BATCH):
                    i = mm(bank[2 + b][:, 2 * t * QUARTER:2 * (t + 1) * QUARTER], oh1[b][:, :, t],
                           oh2g[b][:, :, :, t].rearrange("p w e -> p (w e)"), start=True, stop=True)
                i.then_inc(g_done, 1)

            def up_pair(i, last):
                for b in range(2):
                    m = 4 * i + 2 * b
                    u, ur = U_PRE + 2 * UP_FIRST + 4 * i + 2 * b, U_PRE + 2 * UP_FIRST + 2 * b
                    gate_batch(m, 0)
                    if last and b:
                        gate_batch(m + 1, 1)
                        up(UP_FIRST + 2 * i + b, b, u, ur)
                    else:
                        up(UP_FIRST + 2 * i + b, b, u, ur, lambda: gate_batch(m + 1, 1))

            with pe.Fori(0, UP_LOOPS - 1) as i:
                up_pair(i, False)
            up_pair(UP_LOOPS - 1, True)

            def down(n, par, j, u, ur, free):
                if free:
                    pe.wait_ge(acc_done, n - 1)
                last = isinstance(n, int) and n == GROUPS * GROUP - 1
                for h, blocks in ((0, [0]), (1, [0]), (0, [1]), (1, [1])) if last else ((0, [0, 1]), (1, [0, 1])):
                    wait_lo(pe, u + h, ur + h)
                    if j == 0:
                        pe.wait_ge(clo_done, n + 2 * h + 2)
                    hi_w, lo_w = w_hi[(ur + h) % SPLIT], w_lo[(ur + h) % SPLIT]
                    for e in range(2):
                        w1, w2 = hi_w[:, e * DCH:(e + 1) * DCH], lo_w[:, e * DCH:(e + 1) * DCH]
                        for b in blocks:
                            dst = bank[4 + 2 * (j % 2) + b][:, :]
                            a1 = c_hi[par][:, 2 * h + e, b * P:(b + 1) * P]
                            a2 = c_lo[par][:, 2 * h + e, b * P:(b + 1) * P]
                            mm(dst, a1, w1, start=h == 0 and e == 0, stop=False)
                            mm(dst, a1, w2, start=False, stop=False)
                            i = mm(dst, a2, w1, start=False, stop=h == 1 and e == 1)
                    if 1 in blocks:
                        i.then_inc(used, 1)
                    elif h:
                        i.then_inc(v0_done, 1)

            def group(g, par, ups, builds):
                first = isinstance(g, int) and g == 0
                for j in range(GROUP):
                    if ups:
                        u, ur = U_MAIN + GSTEP * g + STEP * j, U_MAIN + STEP * j
                    else:
                        u, ur = U_TAIL + 2 * GROUP * (g - GROUPS + AHEAD) + 2 * j, U_TAIL + 2 * j
                    down(GROUP * g + j, par % 2, j, u, ur, not (first and j < 2))
                    turn = list(batches(g, j)) if builds else []
                    if len(turn) == 2:
                        gate_batch(turn[0][0], turn[0][4])
                    if ups:
                        up(GROUP * (g + AHEAD) + j, j, u + 2, ur + 2,
                           (lambda: gate_batch(turn[-1][0], turn[-1][4])) if builds else None)

            group(0, 0, True, True)
            with pe.Fori(0, 11) as p:
                for b in range(2):
                    group(2 * p + 1 + b, 1 + b, True, True)
            for g in range(23, GROUPS - AHEAD):
                group(g, g % 2, True, False)
            with pe.Fori((GROUPS - AHEAD) // 2, GROUPS // 2 - 1) as p:
                for b in range(2):
                    group(2 * p + b, b, False, False)
            for g in range(GROUPS - 2, GROUPS):
                group(g, g % 2, False, False)


_OUT_SHAPE = (1, T, D)


def kernel(**inputs):
    import numpy as _np
    import concourse.bacc as _bacc
    from concourse import mybir as _mybir
    from concourse.bass_utils import run_bass_kernel_spmd as _run

    a = {name: _np.asarray(value) for name, value in inputs.items()}
    c, s = CONF_TILES, SC_TILES
    order = [t for i in range(c) for t in (i, c + i)] + [2 * c + t for i in range(s) for t in (s + i, 2 * s + i, i)]

    def stationary_units(w):
        n = w.shape[1] // P
        return w.reshape(2, HALF, P, n, P).transpose(3, 0, 2, 1, 4)

    w_in = stationary_units(a["w_in"][0])[order]
    w_q = stationary_units(a["w_q"][0])
    u_w = a["peer_u"][0].reshape(N_KEYS, N_KEYS, 2, HALF, P).transpose(1, 2, 4, 3, 0)
    v_w = a["peer_v"][0].reshape(N_KEYS, GROUPS, 2, 2, NCH, DCH).transpose(1, 4, 2, 0, 3, 5)
    w_out = a["w_out"][0].reshape(2, 4, 2, P, NCH, DCH).transpose(4, 0, 1, 3, 2, 5)
    w_out = w_out.transpose(1, 0, 2, 3, 4, 5)[::-1]
    cols = [a["b_in"][0].reshape(-1, P)[order].T,
            a["conf_conv_w"][0].reshape(TAPS, c, P).transpose(2, 1, 0).reshape(P, -1),
            a["conf_conv_b"][0].reshape(c, P).T, a["conf_ln_g"][0].reshape(c, P).T, a["conf_ln_b"][0].reshape(c, P).T,
            a["sc_conv_w"][0].reshape(SC_TAPS, s, P).transpose(2, 1, 0).reshape(P, -1),
            a["sc_conv_b"][0].reshape(s, P).T]
    laid = {
        "x_t": a["x"][0].reshape(T, KT, P).transpose(2, 1, 0),
        "x_nat": a["x"][0],
        "w_in": w_in.reshape(-1, P, HALF * P),
        "w_out": w_out.reshape(-1, P, HALF * P),
        "w_q": w_q.reshape(-1, P, HALF * P),
        "u_w": u_w.reshape(-1, P, HALF * P),
        "v_w": v_w.reshape(-1, P, HALF * P),
        "params": _np.concatenate(cols, axis=1),
        "sub_keys": a["sub_keys"][0].transpose(3, 0, 1, 2).reshape(P, -1),
    }
    for name in ("b_out", "ln1_g", "ln1_b", "ln2_g", "ln2_b"):
        laid[name] = a[name].reshape(1, D)

    nc = _bacc.Bacc("TRN2", target_bir_lowering=False, num_devices=1, dynamic_dma_scratch_size=1024)
    arrays, args = {}, []
    for name, value in laid.items():
        value = _np.ascontiguousarray(value)
        arrays[f"in_{name}_dram"] = value
        args.append(nc.dram_tensor(f"in_{name}_dram", value.shape, _mybir.dt.from_np(value.dtype),
                                   kind="ExternalInput").ap())
    args.append(nc.dram_tensor("out_dram", _OUT_SHAPE[1:], _mybir.dt.float32, kind="ExternalOutput").ap())
    build(nc, *args)
    r = _run(nc, [arrays], core_ids=[0])
    return r.results[0]["out_dram"].reshape(_OUT_SHAPE)
```
